# Optimizing a Trainium2 kernel written in Bass

```python
import jax, jax.numpy as jnp
from jax import lax
import numpy as np
import math

D_MODEL = 1024
BATCH = 1
SEQ = 512
DEPTH = 2

N_HEADS = 8
HEAD_DIM = 64
ATTN_WIDTH = N_HEADS * HEAD_DIM
CONV_CH = 512
CONV_K = 31
D_FF = 2816
D_PLE = 256
Q_BLOCK = 128
EPS = 1e-6
FFN_RES = 0.5

Q0 = 0
K0 = Q0 + ATTN_WIDTH
V0 = K0 + ATTN_WIDTH
F0 = V0 + ATTN_WIDTH
C0 = F0 + N_HEADS
GA0 = C0 + 2 * CONV_CH
GC0 = GA0 + D_MODEL
IN_COLS = GC0 + D_MODEL


def rmsnorm(x, g):
    xf = x.astype(jnp.float32)
    y = xf * lax.rsqrt(jnp.mean(xf * xf, axis=-1, keepdims=True) + EPS)
    return (y * g.astype(jnp.float32)).astype(x.dtype)

def swiglu(x, w_in, w_out):
    a, b = jnp.split(x @ w_in, 2, axis=-1)
    return (jax.nn.silu(a) * b) @ w_out

def forgetting_attention(q, k, v, f_logit):
    b, s, h, dh = q.shape
    scale = 1.0 / float(np.sqrt(dh))
    c = jnp.cumsum(jax.nn.log_sigmoid(f_logit.astype(jnp.float32)), axis=1)
    c = jnp.transpose(c, (0, 2, 1))
    qh = jnp.transpose(q, (0, 2, 1, 3))
    kh = jnp.transpose(k, (0, 2, 1, 3))
    vh = jnp.transpose(v, (0, 2, 1, 3))
    outs = []
    for blk in range(s // Q_BLOCK):
        qs, qe = blk * Q_BLOCK, (blk + 1) * Q_BLOCK
        sc = jnp.einsum('bhqd,bhkd->bhqk', qh[:, :, qs:qe], kh[:, :, :qe]).astype(jnp.float32) * scale
        sc = sc + (c[:, :, qs:qe, None] - c[:, :, None, :qe])
        causal = jnp.arange(qs, qe)[:, None] >= jnp.arange(qe)[None, :]
        sc = jnp.where(causal[None, None], sc, -jnp.inf)
        pr = jax.nn.softmax(sc, axis=-1).astype(vh.dtype)
        outs.append(jnp.einsum('bhqk,bhkd->bhqd', pr, vh[:, :, :qe]))
    o = jnp.concatenate(outs, axis=2)
    return jnp.transpose(o, (0, 2, 1, 3)).reshape(b, s, h * dh)

def conformer_conv(glu_in, conv_w, conv_b, g_conv):
    a = glu_in[..., :CONV_CH] * jax.nn.sigmoid(glu_in[..., CONV_CH:])
    y = lax.conv_general_dilated(
        a, conv_w[:, None, :].astype(a.dtype), window_strides=(1,),
        padding=[(CONV_K - 1, 0)], dimension_numbers=('NWC', 'WIO', 'NWC'),
        feature_group_count=CONV_CH) + conv_b
    return jax.nn.silu(rmsnorm(y, g_conv))

def hybrid_mixer(u, w_in, b_f, w_attn_out, conv_w, conv_b, g_conv, w_conv_out, w_out):
    b, s, _ = u.shape
    z = u @ w_in
    q = z[..., Q0:K0].reshape(b, s, N_HEADS, HEAD_DIM)
    k = z[..., K0:V0].reshape(b, s, N_HEADS, HEAD_DIM)
    v = z[..., V0:F0].reshape(b, s, N_HEADS, HEAD_DIM)
    f_logit = z[..., F0:C0] + b_f
    y_attn = forgetting_attention(q, k, v, f_logit) @ w_attn_out
    y_conv = conformer_conv(z[..., C0:GA0], conv_w, conv_b, g_conv) @ w_conv_out
    merged = jax.nn.sigmoid(z[..., GA0:GC0]) * y_attn + jax.nn.sigmoid(z[..., GC0:]) * y_conv
    return merged @ w_out

def first_inputs(seed: int = 0) -> dict:
    key = jax.random.key(seed)
    ks = jax.random.split(key, 24)
    L, D, F = DEPTH, D_MODEL, D_FF
    f32 = jnp.float32

    def w(k, shape, fan_in):
        return jax.random.normal(k, shape, f32) * (fan_in ** -0.5)

    def gain(k, shape):
        return 1.0 + 0.05 * jax.random.normal(k, shape, f32)

    return {
        "x": jax.random.normal(ks[0], (BATCH, SEQ, D), f32),
        "p": jax.random.normal(ks[1], (DEPTH, BATCH, SEQ, D_PLE), f32),
        "g_ff1": gain(ks[2], (L, D)),
        "w_ff1_in": w(ks[3], (L, D, 2 * F), D),
        "w_ff1_out": w(ks[4], (L, F, D), F),
        "g_mix": gain(ks[5], (L, D)),
        "w_in": w(ks[6], (L, D, IN_COLS), D),
        "b_f": 2.0 + 0.5 * jax.random.normal(ks[7], (L, N_HEADS), f32),
        "w_attn_out": w(ks[8], (L, ATTN_WIDTH, D), ATTN_WIDTH),
        "conv_w": w(ks[9], (L, CONV_K, CONV_CH), CONV_K),
        "conv_b": 0.02 * jax.random.normal(ks[10], (L, CONV_CH), f32),
        "g_conv": gain(ks[11], (L, CONV_CH)),
        "w_conv_out": w(ks[12], (L, CONV_CH, D), CONV_CH),
        "w_out": w(ks[13], (L, D, D), D),
        "g_ff2": gain(ks[14], (L, D)),
        "w_ff2_in": w(ks[15], (L, D, 2 * F), D),
        "w_ff2_out": w(ks[16], (L, F, D), F),
        "g_ple": gain(ks[17], (L, D)),
        "w_ple_gate": w(ks[18], (L, D, D), D),
        "w_ple_proj": w(ks[19], (L, D_PLE, D), D_PLE),
        "g_final": gain(ks[20], (D,)),
    }

def first_block(x, p, g_ff1, w_ff1_in, w_ff1_out, g_mix, w_in, b_f, w_attn_out,
              conv_w, conv_b, g_conv, w_conv_out, w_out, g_ff2, w_ff2_in, w_ff2_out,
              g_ple, w_ple_gate, w_ple_proj, g_final):
    h = x
    for i in range(DEPTH):
        h = h + FFN_RES * swiglu(rmsnorm(h, g_ff1[i]), w_ff1_in[i], w_ff1_out[i])
        h = h + hybrid_mixer(rmsnorm(h, g_mix[i]), w_in[i], b_f[i], w_attn_out[i],
                             conv_w[i], conv_b[i], g_conv[i], w_conv_out[i], w_out[i])
        h = h + FFN_RES * swiglu(rmsnorm(h, g_ff2[i]), w_ff2_in[i], w_ff2_out[i])
        gate = jax.nn.sigmoid(rmsnorm(h, g_ple[i]) @ w_ple_gate[i])
        h = h + gate * (p[i] @ w_ple_proj[i])
    return rmsnorm(h, g_final)


DEPTH_2 = 4

N_MIXERS = 4
N_A = (DEPTH_2 + 3) // 4
N_B = (DEPTH_2 + 2) // 4
N_C = (DEPTH_2 + 1) // 4
N_D = DEPTH_2 // 4
NEG_INF = -1e30

SSM_WIDTH = D_MODEL
SSM_GROUP = 16
SSM_GROUPS = SSM_WIDTH // SSM_GROUP
SSM_STATE = 64
DT_MIN = 1e-3
DT_MAX = 1e-1

SWA_HEADS = D_MODEL // HEAD_DIM
SWA_KV_HEADS = SWA_HEADS // 8
SWA_WIDTH = SWA_HEADS * HEAD_DIM
WINDOW = 128

REL_BUCKETS = 32
REL_MAX_DIST = 128

MLA_HEADS = 16
MLA_NOPE = 64
MLA_ROPE = 32
MLA_V = 64
MLA_KV_RANK = 256
MLA_Q_RANK = 768
MLA_WIDTH = MLA_HEADS * MLA_V
ROPE_BASE = 10000.0

SGU_WIDTH = D_MODEL
SGU_CHUNK = 128
SGU_GROUPS = 16
SGU_GROUP_DIM = SGU_WIDTH // SGU_GROUPS


def rmsnorm_2(x, g):
    xf = x.astype(jnp.float32)
    y = xf * lax.rsqrt(jnp.mean(xf * xf, axis=-1, keepdims=True) + EPS)
    return (y * g.astype(jnp.float32)).astype(x.dtype)

def layernorm(x, g, b):
    xf = x.astype(jnp.float32)
    mu = jnp.mean(xf, axis=-1, keepdims=True)
    var = jnp.mean(jnp.square(xf - mu), axis=-1, keepdims=True)
    y = (xf - mu) * lax.rsqrt(var + EPS) * g.astype(jnp.float32) + b.astype(jnp.float32)
    return y.astype(x.dtype)

def _ssm_combine(left, right):
    a1r, a1i, b1r, b1i = left
    a2r, a2i, b2r, b2i = right
    return (a2r * a1r - a2i * a1i,
            a2r * a1i + a2i * a1r,
            a2r * b1r - a2i * b1i + b2r,
            a2r * b1i + a2i * b1r + b2i)

def s5_mixer(u, lam_re, lam_im, log_dt, b_re, b_im, c_re, c_im, d_skip, w_glu, b_glu):
    f32 = jnp.float32
    bsz, L, _ = u.shape
    ug = u.astype(f32).reshape(bsz, L, SSM_GROUPS, SSM_GROUP)
    lr = lam_re.astype(f32)
    li = lam_im.astype(f32)
    dt = jnp.exp(log_dt.astype(f32))[:, None]
    mag = jnp.exp(lr * dt)
    ab_re = mag * jnp.cos(li * dt)
    ab_im = mag * jnp.sin(li * dt)
    den = lr * lr + li * li
    nr = ab_re - 1.0
    f_re = (nr * lr + ab_im * li) / den
    f_im = (ab_im * lr - nr * li) / den
    br = b_re.astype(f32)
    bi = b_im.astype(f32)
    bb_re = f_re[..., None] * br - f_im[..., None] * bi
    bb_im = f_re[..., None] * bi + f_im[..., None] * br
    bu_re = jnp.einsum('blgh,gph->blgp', ug, bb_re)
    bu_im = jnp.einsum('blgh,gph->blgp', ug, bb_im)
    a_re = jnp.broadcast_to(ab_re, (1, L) + ab_re.shape)
    a_im = jnp.broadcast_to(ab_im, (1, L) + ab_im.shape)
    _, _, s_re, s_im = lax.associative_scan(_ssm_combine, (a_re, a_im, bu_re, bu_im), axis=1)
    y = (jnp.einsum('blgp,ghp->blgh', s_re, c_re.astype(f32))
         - jnp.einsum('blgp,ghp->blgh', s_im, c_im.astype(f32)))
    y = y.reshape(bsz, L, SSM_WIDTH) + d_skip.astype(f32) * u.astype(f32)
    y = jax.nn.gelu(y).astype(u.dtype)
    return y * jax.nn.sigmoid(y @ w_glu + b_glu)

def s5_branch(h, w_in, lam_re, lam_im, log_dt, b_re, b_im, c_re, c_im, d_skip, w_glu, b_glu, w_out):
    u, z = jnp.split(h @ w_in, [SSM_WIDTH], axis=-1)
    y = s5_mixer(u, lam_re, lam_im, log_dt, b_re, b_im, c_re, c_im, d_skip, w_glu, b_glu)
    return (y * jax.nn.silu(z)) @ w_out

def t5_bucket(dist):
    max_exact = REL_BUCKETS // 2
    dist_f = jnp.maximum(dist, 1).astype(jnp.float32)
    large = max_exact + (jnp.log(dist_f / max_exact) / math.log(REL_MAX_DIST / max_exact)
                         * (REL_BUCKETS - max_exact)).astype(jnp.int32)
    large = jnp.minimum(large, REL_BUCKETS - 1)
    return jnp.where(dist < max_exact, dist, large)

def sliding_window_attention(q, k, v, sinks, rel_bias):
    bsz, L = q.shape[0], q.shape[1]
    nb = L // WINDOW
    grp = SWA_HEADS // SWA_KV_HEADS
    qb = q.reshape(bsz, nb, WINDOW, SWA_KV_HEADS, grp, HEAD_DIM)

    def band(t):
        prev = jnp.pad(t, ((0, 0), (WINDOW, 0), (0, 0), (0, 0)))[:, :L]
        shp = (bsz, nb, WINDOW, SWA_KV_HEADS, HEAD_DIM)
        return jnp.concatenate([prev.reshape(shp), t.reshape(shp)], axis=2)

    kb = band(k)
    vb = band(v)
    s = jnp.einsum('bnqhgd,bnkhd->bnhgqk', qb, kb).astype(jnp.float32) * (HEAD_DIM ** -0.5)
    qi = jnp.arange(WINDOW)[:, None]
    kj = jnp.arange(2 * WINDOW)[None, :]
    dist = qi + WINDOW - kj
    blk = jnp.arange(nb)[:, None, None]
    valid = (dist >= 0) & (dist < WINDOW) & (blk * WINDOW + kj - WINDOW >= 0)
    bias = rel_bias[t5_bucket(jnp.maximum(dist, 0))]
    bias = jnp.transpose(bias, (2, 0, 1)).reshape(SWA_KV_HEADS, grp, WINDOW, 2 * WINDOW).astype(jnp.float32)
    s = jnp.where(valid[None, :, None, None], s + bias, NEG_INF)
    sink = jnp.broadcast_to(sinks.astype(jnp.float32).reshape(SWA_KV_HEADS, grp, 1, 1), s.shape[:-1] + (1,))
    p = jax.nn.softmax(jnp.concatenate([s, sink], axis=-1), axis=-1)[..., :-1]
    o = jnp.einsum('bnhgqk,bnkhd->bnqhgd', p.astype(v.dtype), vb)
    return o.reshape(bsz, L, SWA_WIDTH)

def swa_branch(h, w_in, sinks, w_out, rel_bias):
    bsz, L, _ = h.shape
    kv_w = SWA_KV_HEADS * HEAD_DIM
    q, k, v, z = jnp.split(h @ w_in, [SWA_WIDTH, SWA_WIDTH + kv_w, SWA_WIDTH + 2 * kv_w], axis=-1)
    q = q.reshape(bsz, L, SWA_HEADS, HEAD_DIM)
    k = k.reshape(bsz, L, SWA_KV_HEADS, HEAD_DIM)
    v = v.reshape(bsz, L, SWA_KV_HEADS, HEAD_DIM)
    o = sliding_window_attention(q, k, v, sinks, rel_bias)
    return (o * jax.nn.silu(z)) @ w_out

def rope_tables(L):
    inv = ROPE_BASE ** (-jnp.arange(0, MLA_ROPE, 2, dtype=jnp.float32) / MLA_ROPE)
    ang = jnp.arange(L, dtype=jnp.float32)[:, None] * inv[None, :]
    return jnp.cos(ang), jnp.sin(ang)

def apply_rope(x, cos, sin):
    xf = x.astype(jnp.float32)
    x1, x2 = jnp.split(xf, 2, axis=-1)
    return jnp.concatenate([x1 * cos - x2 * sin, x2 * cos + x1 * sin], axis=-1).astype(x.dtype)

def causal_block_attention(q, k, v):
    bsz, L, H, dk = q.shape
    nb = L // Q_BLOCK
    scale = dk ** -0.5
    qb = q.reshape(bsz, nb, Q_BLOCK, H, dk).transpose(1, 0, 2, 3, 4)
    kpos = jnp.arange(L)

    def one_block(args):
        qi, n = args
        s = jnp.einsum('bqhd,bkhd->bhqk', qi, k).astype(jnp.float32) * scale
        qpos = n * Q_BLOCK + jnp.arange(Q_BLOCK)
        s = jnp.where(kpos[None, :] <= qpos[:, None], s, NEG_INF)
        p = jax.nn.softmax(s, axis=-1).astype(v.dtype)
        return jnp.einsum('bhqk,bkhd->bqhd', p, v)

    o = lax.map(one_block, (qb, jnp.arange(nb)))
    return o.transpose(1, 0, 2, 3, 4).reshape(bsz, L, H, v.shape[-1])

def mla_branch(h, w_in, q_norm, kv_norm, w_uq, w_ukv, w_out):
    bsz, L, _ = h.shape
    c_q, c_kv, k_rope, z = jnp.split(
        h @ w_in, [MLA_Q_RANK, MLA_Q_RANK + MLA_KV_RANK, MLA_Q_RANK + MLA_KV_RANK + MLA_ROPE], axis=-1)
    q = (rmsnorm_2(c_q, q_norm) @ w_uq).reshape(bsz, L, MLA_HEADS, MLA_NOPE + MLA_ROPE)
    kv = (rmsnorm_2(c_kv, kv_norm) @ w_ukv).reshape(bsz, L, MLA_HEADS, MLA_NOPE + MLA_V)
    cos, sin = rope_tables(L)
    q = jnp.concatenate([q[..., :MLA_NOPE], apply_rope(q[..., MLA_NOPE:], cos[:, None], sin[:, None])], axis=-1)
    k_rope = apply_rope(k_rope, cos, sin)
    k = jnp.concatenate([kv[..., :MLA_NOPE],
                         jnp.broadcast_to(k_rope[:, :, None, :], (bsz, L, MLA_HEADS, MLA_ROPE))], axis=-1)
    o = causal_block_attention(q, k, kv[..., MLA_NOPE:])
    return (o.reshape(bsz, L, MLA_WIDTH) * jax.nn.silu(z)) @ w_out

def sgu_branch(h, w_in, ln_g, ln_b, w_s, b_s, w_out):
    bsz, L, _ = h.shape
    uv, z = jnp.split(h @ w_in, [2 * SGU_WIDTH], axis=-1)
    u, v = jnp.split(jax.nn.gelu(uv), 2, axis=-1)
    v = layernorm(v, ln_g, ln_b).reshape(bsz, L // SGU_CHUNK, SGU_CHUNK, SGU_GROUPS, SGU_GROUP_DIM)
    tril = jnp.tril(jnp.ones((SGU_CHUNK, SGU_CHUNK), dtype=bool))
    w = jnp.where(tril[None], w_s, 0.0)
    s = jnp.einsum('gts,bnsgc->bntgc', w, v) + b_s.T[:, :, None]
    s = s.reshape(bsz, L, SGU_WIDTH)
    return (u * s * jax.nn.silu(z)) @ w_out

def second_inputs(seed: int = 0) -> dict:
    key = jax.random.key(seed)
    ks = iter(jax.random.split(key, 40))
    f32 = jnp.float32

    def nrm(shape, scale):
        return jax.random.normal(next(ks), shape, f32) * scale

    x = nrm((BATCH, SEQ, D_MODEL), 1.0)
    pre_norm = 1.0 + nrm((DEPTH_2, D_MODEL), 0.05)
    post_norm = 1.0 + nrm((DEPTH_2, D_MODEL), 0.05)
    rel_bias = nrm((REL_BUCKETS, SWA_HEADS), 0.5)
    a_w_in = nrm((N_A, D_MODEL, 2 * SSM_WIDTH), D_MODEL ** -0.5)
    n_idx = jnp.arange(SSM_STATE, dtype=f32)
    a_lam_re = -0.5 + nrm((N_A, SSM_GROUPS, SSM_STATE), 0.01)
    a_lam_im = jnp.pi * n_idx + nrm((N_A, SSM_GROUPS, SSM_STATE), 0.01)
    a_log_dt = jax.random.uniform(next(ks), (N_A, SSM_GROUPS), f32, math.log(DT_MIN), math.log(DT_MAX))
    a_b_re = nrm((N_A, SSM_GROUPS, SSM_STATE, SSM_GROUP), (2 * SSM_GROUP) ** -0.5)
    a_b_im = nrm((N_A, SSM_GROUPS, SSM_STATE, SSM_GROUP), (2 * SSM_GROUP) ** -0.5)
    a_c_re = nrm((N_A, SSM_GROUPS, SSM_GROUP, SSM_STATE), SSM_STATE ** -0.5)
    a_c_im = nrm((N_A, SSM_GROUPS, SSM_GROUP, SSM_STATE), SSM_STATE ** -0.5)
    a_d = nrm((N_A, SSM_WIDTH), 1.0)
    a_w_glu = nrm((N_A, SSM_WIDTH, SSM_WIDTH), SSM_WIDTH ** -0.5)
    a_b_glu = nrm((N_A, SSM_WIDTH), 0.02)
    a_w_out = nrm((N_A, SSM_WIDTH, D_MODEL), SSM_WIDTH ** -0.5)
    b_w_in = nrm((N_B, D_MODEL, 2 * SWA_WIDTH + 2 * SWA_KV_HEADS * HEAD_DIM), D_MODEL ** -0.5)
    b_sinks = nrm((N_B, SWA_HEADS), 1.0)
    b_w_out = nrm((N_B, SWA_WIDTH, D_MODEL), SWA_WIDTH ** -0.5)
    c_w_in = nrm((N_C, D_MODEL, MLA_Q_RANK + MLA_KV_RANK + MLA_ROPE + MLA_WIDTH), D_MODEL ** -0.5)
    c_q_norm = 1.0 + nrm((N_C, MLA_Q_RANK), 0.05)
    c_kv_norm = 1.0 + nrm((N_C, MLA_KV_RANK), 0.05)
    c_w_uq = nrm((N_C, MLA_Q_RANK, MLA_HEADS * (MLA_NOPE + MLA_ROPE)), MLA_Q_RANK ** -0.5)
    c_w_ukv = nrm((N_C, MLA_KV_RANK, MLA_HEADS * (MLA_NOPE + MLA_V)), MLA_KV_RANK ** -0.5)
    c_w_out = nrm((N_C, MLA_WIDTH, D_MODEL), MLA_WIDTH ** -0.5)
    d_w_in = nrm((N_D, D_MODEL, 3 * SGU_WIDTH), D_MODEL ** -0.5)
    d_ln_g = 1.0 + nrm((N_D, SGU_WIDTH), 0.05)
    d_ln_b = nrm((N_D, SGU_WIDTH), 0.02)
    d_w_s = nrm((N_D, SGU_GROUPS, SGU_CHUNK, SGU_CHUNK), 0.5 * SGU_CHUNK ** -0.5)
    d_b_s = 1.0 + nrm((N_D, SGU_GROUPS, SGU_CHUNK), 0.1)
    d_w_out = nrm((N_D, SGU_WIDTH, D_MODEL), SGU_WIDTH ** -0.5)
    return {'x': x, 'pre_norm': pre_norm, 'post_norm': post_norm, 'rel_bias': rel_bias,
            'a_w_in': a_w_in, 'a_lam_re': a_lam_re, 'a_lam_im': a_lam_im, 'a_log_dt': a_log_dt,
            'a_b_re': a_b_re, 'a_b_im': a_b_im, 'a_c_re': a_c_re, 'a_c_im': a_c_im, 'a_d': a_d,
            'a_w_glu': a_w_glu, 'a_b_glu': a_b_glu, 'a_w_out': a_w_out,
            'b_w_in': b_w_in, 'b_sinks': b_sinks, 'b_w_out': b_w_out,
            'c_w_in': c_w_in, 'c_q_norm': c_q_norm, 'c_kv_norm': c_kv_norm, 'c_w_uq': c_w_uq,
            'c_w_ukv': c_w_ukv, 'c_w_out': c_w_out,
            'd_w_in': d_w_in, 'd_ln_g': d_ln_g, 'd_ln_b': d_ln_b, 'd_w_s': d_w_s, 'd_b_s': d_b_s,
            'd_w_out': d_w_out}

def second_block(x, pre_norm, post_norm, rel_bias,
              a_w_in, a_lam_re, a_lam_im, a_log_dt, a_b_re, a_b_im, a_c_re, a_c_im, a_d,
              a_w_glu, a_b_glu, a_w_out,
              b_w_in, b_sinks, b_w_out,
              c_w_in, c_q_norm, c_kv_norm, c_w_uq, c_w_ukv, c_w_out,
              d_w_in, d_ln_g, d_ln_b, d_w_s, d_b_s, d_w_out):
    for i in range(DEPTH_2):
        kind = i % N_MIXERS
        j = i // N_MIXERS
        h = rmsnorm_2(x, pre_norm[i])
        if kind == 0:
            y = s5_branch(h, a_w_in[j], a_lam_re[j], a_lam_im[j], a_log_dt[j], a_b_re[j], a_b_im[j],
                          a_c_re[j], a_c_im[j], a_d[j], a_w_glu[j], a_b_glu[j], a_w_out[j])
        elif kind == 1:
            y = swa_branch(h, b_w_in[j], b_sinks[j], b_w_out[j], rel_bias)
        elif kind == 2:
            y = mla_branch(h, c_w_in[j], c_q_norm[j], c_kv_norm[j], c_w_uq[j], c_w_ukv[j], c_w_out[j])
        else:
            y = sgu_branch(h, d_w_in[j], d_ln_g[j], d_ln_b[j], d_w_s[j], d_b_s[j], d_w_out[j])
        x = x + rmsnorm_2(y, post_norm[i])
    return x


_first_inputs = second_inputs


def second_inputs(seed=0):
    import zlib

    import numpy as np

    out = dict(_first_inputs(seed))
    spreads = {}
    factors = {'a_lam_re': 8.0, 'a_b_glu': 5.028, 'c_q_norm': 3.589, 'd_ln_g': 7.844, 'd_ln_b': 8.0}
    for name, (base, spread) in spreads.items():
        noise = np.random.default_rng([zlib.crc32(name.encode()), seed]).standard_normal(out[name].shape)
        drawn = base * np.exp(spread * noise) if base else spread * noise
        out[name] = __import__('jax').numpy.asarray(drawn.astype(out[name].dtype))
    for name, factor in factors.items():
        out[name] = (out[name] * factor).astype(out[name].dtype)
    return out


_narrow_inputs = second_inputs


def second_inputs(seed=0):
    out = dict(_narrow_inputs(seed))
    wider = {'a_lam_re': 12.0, 'd_ln_g': 3.29, 'd_ln_b': 8.55, 'd_b_s': 3.35}
    for name, times in wider.items():
        mean = out[name].mean()
        out[name] = (mean + times * (out[name] - mean)).astype(out[name].dtype)
    return out


def setup_inputs(seed=0):
    out = dict(first_inputs(seed))
    for name, value in second_inputs(seed + 1).items():
        if name != "x":
            out[name + "_2"] = value
    return out


def reference(
    x, p, g_ff1, w_ff1_in, w_ff1_out, g_mix, w_in, b_f, w_attn_out, conv_w, conv_b, g_conv,
    w_conv_out, w_out, g_ff2, w_ff2_in, w_ff2_out, g_ple, w_ple_gate, w_ple_proj, g_final,
    pre_norm_2, post_norm_2, rel_bias_2, a_w_in_2, a_lam_re_2, a_lam_im_2, a_log_dt_2, a_b_re_2,
    a_b_im_2, a_c_re_2, a_c_im_2, a_d_2, a_w_glu_2, a_b_glu_2, a_w_out_2, b_w_in_2, b_sinks_2,
    b_w_out_2, c_w_in_2, c_q_norm_2, c_kv_norm_2, c_w_uq_2, c_w_ukv_2, c_w_out_2, d_w_in_2,
    d_ln_g_2, d_ln_b_2, d_w_s_2, d_b_s_2, d_w_out_2,
):
    x = first_block(
        x, p, g_ff1, w_ff1_in, w_ff1_out, g_mix, w_in, b_f, w_attn_out, conv_w, conv_b, g_conv,
        w_conv_out, w_out, g_ff2, w_ff2_in, w_ff2_out, g_ple, w_ple_gate, w_ple_proj, g_final,
    )
    return second_block(
        x, pre_norm_2, post_norm_2, rel_bias_2, a_w_in_2, a_lam_re_2, a_lam_im_2, a_log_dt_2,
        a_b_re_2, a_b_im_2, a_c_re_2, a_c_im_2, a_d_2, a_w_glu_2, a_b_glu_2, a_w_out_2,
        b_w_in_2, b_sinks_2, b_w_out_2, c_w_in_2, c_q_norm_2, c_kv_norm_2, c_w_uq_2, c_w_ukv_2,
        c_w_out_2, d_w_in_2, d_ln_g_2, d_ln_b_2, d_w_s_2, d_b_s_2, d_w_out_2,
    )


_drawn_inputs = setup_inputs


def setup_inputs(seed=0):
    import zlib

    import numpy as np

    out = dict(_drawn_inputs(seed))
    spreads = {}
    factors = {}
    for name, (base, spread) in spreads.items():
        noise = np.random.default_rng([zlib.crc32(name.encode()), seed]).standard_normal(out[name].shape)
        drawn = base * np.exp(spread * noise) if base else spread * noise
        out[name] = __import__('jax').numpy.asarray(drawn.astype(out[name].dtype))
    for name, factor in factors.items():
        out[name] = (out[name] * factor).astype(out[name].dtype)
    return out
```

```python
from contextlib import ExitStack, contextmanager

import concourse.bass as bass
import numpy as np
from concourse import mybir

F32 = mybir.dt.float32
F32R = mybir.dt.float32r
BF16 = mybir.dt.bfloat16
I32 = mybir.dt.int32
ALU = mybir.AluOpType
ACT = mybir.ActivationFunctionType
AX = mybir.AxisListType

P = 128
RAW_SLOTS = 4
SPLIT_SLOTS = 2
UNIT_K = 8
EPS = 1e-6
MASKED = -1e30

SEQ = 512
D = 1024
DC = D // P
TT = SEQ // P
HEADS, HD = 8, 64
ATTN = HEADS * HD
CONV_CH, CONV_K = 512, 31
CC = CONV_CH // P
FF = 2816
FC = FF // P
PLE = 256

GROUP, GROUPS, STATE = 16, 64, 64
ST = GROUPS * STATE // P
SWA_HEADS = 16
WINDOW = 128
MLA_HEADS, NOPE, ROPE, MLA_V = 16, 64, 32, 64
KV_RANK, Q_RANK = 256, 768
QK = NOPE + ROPE
SGU_GROUPS = 16
ROUND = 1.5 * 2.0 ** 23
TWO_PI = 2.0 * np.pi


class Signal:

    def __init__(self, handle):
        self.sem = handle
        self.total = 0

    def reserve(self, n):
        base = self.total
        self.total += n
        return base


class Order:

    def __init__(self, handle):
        self.sem = handle
        self.n = 0
        self.loop = None
        self.last = None

    def value(self):
        return self.n if self.loop is None else self.loop[0] * self.loop[1] + self.n

    def next(self):
        self.n += 1
        self.last = (self.sem, self.value())
        return self.sem, 1

    def gives(self, sem, value):
        self.last = (sem, value)
        return sem, 1

    def enter(self, i, per):
        self.loop = (i, per, self.n)
        self.last = (self.sem, self.value())

    def leave(self, iters):
        i, per, n0 = self.loop
        assert self.n - n0 == per, (self.n - n0, per)
        self.loop = None
        self.n = n0 + per * iters
        self.last = (self.sem, self.n)


@contextmanager
def repeat(eng, iters):
    if iters == 1:
        yield 0
    else:
        with eng.Fori(0, iters) as i:
            yield i


def chunks(ap):
    return ap.rearrange("(c p) n -> p c n", p=P)


class Machine:

    def __init__(self, nc, ctx):
        self.nc, self.ctx = nc, ctx
        sem = lambda n: Signal(ctx.enter_context(nc.semaphore(n)))
        self.raw_ready = [ctx.enter_context(nc.semaphore(f"raw_ready{i}")) for i in range(RAW_SLOTS)]
        self.high_ready = sem("high_ready")
        self.low_ready = sem("low_ready")
        self.unit_done = sem("unit_done")
        self.acc_free = [ctx.enter_context(nc.semaphore(f"acc_free{i}")) for i in range(2)]
        self.act_out = sem("act_out")
        self.splits = sem("splits")
        self.squares = sem("squares")
        self.stat = sem("stat")
        self.root = sem("root")
        self.vec = Order(ctx.enter_context(nc.semaphore("vec_order")))
        self.sca = Order(ctx.enter_context(nc.semaphore("sca_order")))
        self.units = 0
        self.tiles = 0
        self.act_tiles = self.act_out.reserve(2) + 2
        self.unit_k = []
        self.raw_total = [0] * RAW_SLOTS
        self.raw_value = []

        sb = self.sb
        self.X = sb("X", [P, DC, SEQ])
        self.UH = sb("UH", [P, DC, SEQ], F32R)
        self.UL = sb("UL", [P, DC, SEQ], F32R)
        self.RAW = sb("RAW", [P, RAW_SLOTS, UNIT_K, P])
        self.WH = sb("WH", [P, SPLIT_SLOTS, UNIT_K, P], F32R)
        self.WL = sb("WL", [P, SPLIT_SLOTS, UNIT_K, P], F32R)
        self.R = sb("R", [P, SEQ])
        self.ROOT = sb("ROOT", [P, SEQ])
        self.SQ = sb("SQ", [P, SEQ])
        self.SS = sb("SS", [P, SEQ])
        self.PRE = sb("PRE", [P, 2, SEQ])
        self.FUN = sb("FUN", [P, 2, SEQ])
        self.T = sb("T", [P, SEQ])
        self.T2 = sb("T2", [P, SEQ])
        self.ONES = sb("ONES", [P, P])
        self.IDENT = sb("IDENT", [P, P])
        self.EPSC = sb("EPSC", [P, 1])
        self.ZERO = sb("ZERO", [P, 1])
        self.ps = ctx.enter_context(nc.psum_tensor("ps", [P, 8, SEQ], F32))

    def sb(self, name, shape, dt=F32, ctx=None):
        return (ctx or self.ctx).enter_context(self.nc.sbuf_tensor(name, shape, dt))


class Step:

    def sync(self, e): pass
    def scalar(self, e): pass
    def gpsimd(self, e): pass
    def vector(self, e): pass
    def tensor(self, e): pass


class Tile:

    def __init__(self, units, rhs, vec=None, act=None, cols=P, pre=None, loads=1):
        self.units, self.rhs, self.vec, self.act, self.cols = units, rhs, vec, act, cols
        self.pre, self.loads = pre, loads


class Gemm(Step):

    needs = ()

    def __init__(self, m, iters, tiles, vec_per_iter=0, rhs_ready=0, splits=0, squares=0, root=None):
        self.m, self.iters, self.body, self.vper = m, iters, tiles, vec_per_iter
        self.rhs_ready, self.root = rhs_ready, root
        self.u0, self.t0, self.a0 = m.units, m.tiles, m.act_tiles
        self.nu = sum(len(t.units) for t in tiles)
        self.nt, self.na = len(tiles), sum(t.act is not None for t in tiles)
        assert iters == 1 or (self.nu % RAW_SLOTS == 0 and self.nt % 2 == 0 and self.na % 2 == 0), (self.nu, self.nt, self.na)
        m.units += iters * self.nu
        m.tiles += iters * self.nt
        m.act_tiles += iters * self.na
        for _ in range(iters):
            for t in tiles:
                for u in t.units:
                    slot = len(m.unit_k) % RAW_SLOTS
                    m.unit_k.append(u[1])
                    m.raw_total[slot] += 16 * t.loads
                    m.raw_value.append(m.raw_total[slot])
                    assert iters == 1 or t.loads == 1
        m.act_out.reserve(iters * self.na)
        self.splits_per, self.squares_per = splits, squares
        self.s0 = m.splits.reserve(iters * splits)
        self.q0 = m.squares.reserve(iters * squares)

    def unit(self, i, j):
        return self.u0 + j + i * self.nu

    def walk(self):
        j = a = 0
        for n, t in enumerate(self.body):
            yield t, n, j, a
            j += len(t.units)
            a += t.act is not None

    def free(self, i, n):
        return 1 + (self.t0 + n) // 2 + i * (self.nt // 2)

    def bank(self, n):
        return (self.t0 + n) % 2

    def sync(self, e):
        m = self.m
        with repeat(e, self.iters) as i:
            j = 0
            for t in self.body:
                for src, k, _ in t.units:
                    u, slot = self.unit(i, j), (self.u0 + j) % RAW_SLOTS
                    e.wait_ge(m.low_ready.sem, u + 1)
                    at_ = 0
                    parts = src(i) if t.loads > 1 else [src(i)]
                    assert len(parts) == t.loads
                    for part in parts:
                        n = part.shape[-1]
                        e.dma_start(m.RAW[:, slot, 0:k, at_:at_ + n], part).then_inc(m.raw_ready[slot], 16)
                        at_ += n
                    j += 1

    def gpsimd(self, e):
        m = self.m
        with repeat(e, self.iters) as i:
            j = 0
            for t in self.body:
                for src, k, _ in t.units:
                    u = self.unit(i, j)
                    r, s = (self.u0 + j) % RAW_SLOTS, (self.u0 + j) % SPLIT_SLOTS
                    e.wait_ge(m.high_ready.sem, u + 1)
                    e.tensor_tensor(m.WL[:, s, 0:k, :], m.RAW[:, r, 0:k, :], m.WH[:, s, 0:k, :].bitcast(F32),
                                    ALU.subtract).then_inc(m.low_ready.sem, 1)
                    self.gpsimd_tail(e, i, j)
                    j += 1

    def high(self, e, i, j):
        m = self.m
        last = self.u0 + self.nu * self.iters
        if j == self.nu:
            k = [m.unit_k[self.u0]] if self.iters > 1 else []
            k += [m.unit_k[last]] if last < len(m.unit_k) else []
            if not k:
                return
            k = max(k)
        else:
            k = m.unit_k[self.u0 + j]
        g = self.u0 + j
        r, s = g % RAW_SLOTS, g % SPLIT_SLOTS
        rounds = i * (self.nu // RAW_SLOTS)
        e.wait_ge(m.raw_ready[r], m.raw_value[g] + rounds * 16)
        e.wait_ge(m.unit_done.sem, self.unit(i, j))
        e.activation(m.WH[:, s, 0:k, :], m.RAW[:, r, 0:k, :], ACT.Copy).then_inc(m.high_ready.sem, 1)

    def scalar(self, e):
        m = self.m
        if self.root is not None:
            self.root.scalar(e)
        with repeat(e, self.iters) as i:
            for t, n, j, a in self.walk():
                for x in range(len(t.units)):
                    if self.iters > 1 or self.u0 + j + x + 1 < len(m.unit_k):
                        self.high(e, i, j + x + 1)
                if t.act is not None:
                    a = self.a0 + a
                    e.wait_ge(m.acc_free[self.bank(n)], self.free(i, n) + 1)
                    t.act(e, i, m.PRE[:, a % 2, :], m.FUN[:, a % 2, :]).then_inc(m.act_out.sem, 1)
                self.scalar_tail(e, i, n)

    def tensor(self, e):
        m = self.m
        if self.root is not None:
            self.root.tensor(e)
        for sem, value in self.needs:
            e.wait_ge(sem, value)
        with repeat(e, self.iters) as i:
            for t, n, j, a in self.walk():
                b = self.bank(n)
                e.wait_ge(m.acc_free[b], self.free(i, n))
                out = m.ps[0:t.cols, b, :]
                H, L = t.rhs
                for x, (src, k, k0) in enumerate(t.units):
                    s = (self.u0 + j + x) % SPLIT_SLOTS
                    u = self.unit(i, j + x)
                    e.wait_ge(m.high_ready.sem, u + 1)
                    for c in range(k):
                        if n == 0 or self.iters == 1:
                            e.wait_ge(m.splits.sem, self.rhs_ready + k0 + c + 1)
                        e.matmul(out, m.WH[:, s, c, 0:t.cols], H[:, k0 + c, :], start=(x == 0 and c == 0), stop=False)
                        e.matmul(out, m.WH[:, s, c, 0:t.cols], L[:, k0 + c, :], start=False, stop=False)
                    e.wait_ge(m.low_ready.sem, u + 1 + RAW_SLOTS)
                    for c in range(k):
                        last = x == len(t.units) - 1 and c == k - 1
                        mm = e.matmul(out, m.WL[:, s, c, 0:t.cols], H[:, k0 + c, :], start=False, stop=last)
                    mm.then_inc(m.unit_done.sem, 1)

    def vector(self, e):
        m = self.m
        if self.root is not None:
            self.root.vector(e)
        with repeat(e, self.iters) as i:
            if self.iters > 1:
                m.vec.enter(i, self.vper)
                if self.splits_per:
                    m.vec.last = (m.splits.sem, self.s0 + i * self.splits_per)
                elif self.squares_per:
                    m.vec.last = (m.squares.sem, self.q0 + i * self.squares_per)
            self.si = self.qi = 0
            for t, n, j, a in self.walk():
                b = self.bank(n)
                e.wait_ge(m.unit_done.sem, self.unit(i, j + len(t.units)) + 1)
                self.i, self.freed = i, (m.acc_free[b], self.free(i, n) + 1)
                self.a = self.a0 + a + i * self.na
                ps = m.ps[0:t.cols, b, :]
                if t.act is not None:
                    ga = self.a0 + a
                    e.wait_ge(m.act_out.sem, self.a - 1)
                    pre = m.PRE[0:t.cols, ga % 2, :]
                    ins = t.pre(e, i, pre, ps) if t.pre else e.tensor_tensor(pre, ps, m.R[0:t.cols, :], ALU.mult)
                    ins.then_inc(m.acc_free[b], 1)
                    m.vec.last = self.freed
                    self.fun = m.FUN[0:t.cols, ga % 2, :]
                    if t.vec is not None:
                        e.wait_ge(m.act_out.sem, self.a + 1)
                        t.vec(self, e, i, None)
                else:
                    t.vec(self, e, i, ps)
                self.vector_tail(e, i, n)
            assert self.si == self.splits_per and self.qi == self.squares_per, (self.si, self.qi)
            if self.iters > 1:
                m.vec.leave(self.iters)
        m.wait_tiles(e, self.t0 + self.nt * self.iters)

    def vector_tail(self, e, i, n):
        pass

    def gpsimd_tail(self, e, i, j):
        pass

    def scalar_tail(self, e, i, n):
        pass

    def frees(self):
        self.m.vec.last = self.freed
        return self.freed[0], 1

    def split(self, e, high, low, src):
        v = self.m.vec
        e.wait_ge(*v.last)
        e.tensor_copy(high, src).then_inc(*v.next())
        e.wait_ge(*v.last)
        self.si += 1
        e.tensor_tensor(low, src, high.bitcast(F32), ALU.subtract).then_inc(*v.gives(self.m.splits.sem, self.s0 + self.i * self.splits_per + self.si))

    def split_gain(self, e, high, low, src, gain):
        v = self.m.vec
        e.wait_ge(*v.last)
        e.tensor_scalar(high, src, gain, None, ALU.mult).then_inc(*v.next())
        e.wait_ge(*v.last)
        self.si += 1
        e.scalar_tensor_tensor(low, src, gain, high.bitcast(F32), ALU.mult, ALU.subtract).then_inc(*v.gives(self.m.splits.sem, self.s0 + self.i * self.splits_per + self.si))

    def square(self, e, src):
        m, v = self.m, self.m.vec
        e.wait_ge(*v.last)
        e.tensor_tensor(m.SQ[:], src, src, ALU.mult).then_inc(*v.next())
        e.wait_ge(*v.last)
        self.qi += 1
        e.tensor_tensor(m.SS[:], m.SS[:], m.SQ[:], ALU.add).then_inc(*v.gives(m.squares.sem, self.q0 + self.i * self.squares_per + self.qi))

    def residual(self, e, i, ps, alpha, gain):
        m = self.m
        x = m.X[:, i, :] if isinstance(i, int) else m.X[:, bass.ds(i, 1), :]
        e.scalar_tensor_tensor(x, ps, alpha, x, ALU.mult, ALU.add).then_inc(*self.frees())
        after_x(self, e, i, gain)


def at(buf, i):
    if isinstance(i, int):
        return buf[:, i, :]
    return buf[:, bass.ds(i, 1), :]


def after_x(g, e, i, gain):
    m = g.m
    x = at(m.X, i)
    g.square(e, x)
    g.split_gain(e, at(m.UH, i), at(m.UL, i), x, gain)


class Root(Step):

    def __init__(self, m, n, need=None, dest=None):
        self.m, self.n = m, n
        self.dest = m.R if dest is None else dest
        self.need = m.squares.total if need is None else need
        self.b = m.stat.reserve(1)
        self.rb = m.root.reserve(1)

    def tensor(self, e):
        m = self.m
        e.wait_ge(m.squares.sem, self.need)
        e.matmul(m.ps[:, 7, :], m.ONES[:], m.SS[:], start=True, stop=True).then_inc(m.stat.sem, 1)

    def scalar(self, e):
        m = self.m
        e.wait_ge(m.stat.sem, self.b + 1)
        e.activation(m.ROOT[:], m.ps[:, 7, :], ACT.Sqrt, bias=m.EPSC[:, 0:1], scale=1.0 / self.n).then_inc(m.root.sem, 1)

    def vector(self, e):
        m, v = self.m, self.m.vec
        e.wait_ge(m.root.sem, self.rb + 1)
        e.wait_ge(*v.last)
        e.memset(m.SS[:], 0.0).then_inc(*v.next())
        e.reciprocal(self.dest[:], m.ROOT[:]).then_inc(*v.next())
        e.wait_ge(*v.last)


class Flips(Step):

    def __init__(self, m, groups, needs=(), splits=0, squares=0, tiles_out=True):
        self.m, self.groups, self.needs = m, groups, list(needs)
        self.b = m.flips.reserve(len(groups))
        self.s0, self.splits_n = m.splits.reserve(splits), splits
        self.q0, self.squares_n = m.squares.reserve(squares), squares
        self.splits_per = self.squares_per = 0
        self.act0 = m.act_out.total
        self.t0 = m.tiles if tiles_out else 0

    def tensor(self, e):
        m = self.m
        for sem, value in self.needs:
            e.wait_ge(sem, value)
        m.wait_tiles(e, self.t0)
        for g, (pe, _) in enumerate(self.groups):
            if self.b + g - 1 > 0:
                e.wait_ge(m.flip_free.sem, self.b + g - 1)
            pe(e, m.ps[:, 4 + (self.b + g) % 2, :]).then_inc(m.flips.sem, 1)

    def vector(self, e):
        m = self.m
        self.i = self.si = self.qi = 0
        for g, (_, vec) in enumerate(self.groups):
            e.wait_ge(m.flips.sem, self.b + g + 1)
            self.freed = (m.flip_free.sem, self.b + g + 1)
            vec(self, e, m.ps[:, 4 + (self.b + g) % 2, :])
        e.wait_ge(*m.vec.last)
        assert (self.si, self.qi) == (self.splits_n, self.squares_n), (self.si, self.qi)

    frees = Gemm.frees
    split = Gemm.split
    split_gain = Gemm.split_gain
    square = Gemm.square


class VectorStep(Step):

    def __init__(self, m, body, asks=(), splits=0, squares=0, root=None, needs=()):
        self.m, self.body, self.asks, self.needs = m, body, list(asks), list(needs)
        self.a0 = m.ask.reserve(len(self.asks))
        self.k0 = m.answer.reserve(len(self.asks))
        self.s0, self.splits_n = m.splits.reserve(splits), splits
        self.root = root
        self.q0, self.squares_n = m.squares.reserve(squares), squares
        self.splits_per = self.squares_per = 0

    def tensor(self, e):
        if self.root is not None:
            self.root.tensor(e)

    def scalar(self, e):
        m = self.m
        if self.root is not None:
            self.root.scalar(e)
        for n, ask in enumerate(self.asks):
            e.wait_ge(m.ask.sem, self.a0 + n + 1)
            ask(e).then_inc(m.answer.sem, 1)

    def vector(self, e):
        m = self.m
        if self.root is not None:
            self.root.vector(e)
        for sem, value in self.needs:
            e.wait_ge(sem, value)
        self.i = self.si = self.qi = self.asked = 0
        e.wait_ge(*m.vec.last)
        self.body(self, e)
        e.wait_ge(*m.vec.last)
        assert (self.si, self.qi) == (self.splits_n, self.squares_n), (self.si, self.qi)
        assert self.asked == len(self.asks)

    def asks_next(self):
        self.asked += 1
        self.m.vec.last = (self.m.ask.sem, self.a0 + self.asked)
        return self.m.ask.sem, 1

    def answered(self, n):
        return self.k0 + n + 1

    split = Gemm.split
    split_gain = Gemm.split_gain
    square = Gemm.square


class Renorm(Step):

    def __init__(self, m, gain, next_gain, y):
        self.m, self.gain, self.next_gain, self.y = m, gain, next_gain, y
        n = 0 if next_gain is None else DC
        self.root = Root(m, D)
        self.x0 = m.x_new.reserve(DC)
        self.h0 = m.x_high.reserve(n)
        self.r0 = m.x_squared.reserve(n)
        self.s0, self.q0 = m.splits.reserve(n), m.squares.reserve(n)

    def tensor(self, e):
        self.root.tensor(e)

    def scalar(self, e):
        m = self.m
        self.root.scalar(e)
        if self.next_gain is None:
            return
        for c in range(DC):
            e.wait_ge(m.x_new.sem, self.x0 + c + 1)
            e.activation(m.UH[:, c, :], m.X[:, c, :], ACT.Copy, scale=self.next_gain(c)).then_inc(m.x_high.sem, 1)
            if c > 1:
                e.wait_ge(m.squares.sem, self.q0 + c - 1)
            e.activation((m.SQ, m.T2)[c % 2][:], m.X[:, c, :], ACT.Square).then_inc(m.x_squared.sem, 1)

    def gpsimd(self, e):
        m = self.m
        if self.next_gain is None:
            return
        for c in range(DC):
            e.wait_ge(m.x_squared.sem, self.r0 + c + 1)
            e.wait_ge(m.squares.sem, self.q0 + c)
            e.tensor_tensor(m.SS[:], m.SS[:], (m.SQ, m.T2)[c % 2][:], ALU.add).then_inc(m.squares.sem, 1)

    def vector(self, e):
        m, v = self.m, self.m.vec
        self.root.vector(e)

        def low(c):
            e.wait_ge(m.x_high.sem, self.h0 + c + 1)
            e.scalar_tensor_tensor(m.UL[:, c, :], m.X[:, c, :], self.next_gain(c), m.UH[:, c, :].bitcast(F32),
                                   ALU.mult, ALU.subtract).then_inc(*v.gives(m.splits.sem, self.s0 + c + 1))

        for c in range(DC):
            e.wait_ge(*v.last)
            x = m.X[:, c, :]
            if self.y is None:
                e.scalar_tensor_tensor(x, x, self.gain(c), m.R[:], ALU.mult, ALU.mult).then_inc(*v.gives(m.x_new.sem, self.x0 + c + 1))
            else:
                e.scalar_tensor_tensor(m.T[:], self.y[:, c, :], self.gain(c), m.R[:], ALU.mult, ALU.mult).then_inc(*v.next())
                if c > 0 and self.next_gain is not None:
                    e.wait_ge(m.x_new.sem, self.x0 + c)
                    low(c - 1)
                e.wait_ge(v.sem, v.n)
                e.tensor_tensor(x, x, m.T[:], ALU.add).then_inc(*v.gives(m.x_new.sem, self.x0 + c + 1))
            if self.y is None and self.next_gain is not None and c > 0:
                e.wait_ge(m.x_new.sem, self.x0 + c)
                low(c - 1)
                if c < DC - 1:
                    v.last = (m.x_new.sem, self.x0 + c + 1)
        if self.next_gain is not None:
            e.wait_ge(m.x_new.sem, self.x0 + DC)
            low(DC - 1)
        e.wait_ge(*v.last)


class Attention(Step):

    def __init__(self, m, buf, heads, q, k, v, out, scale, bias=None, mask=None, sink=None,
                 blocks=lambda n: n + 1, needs=(), splits=0):
        self.m, self.buf, self.heads = m, buf, heads
        self.q, self.k, self.v, self.out, self.scale = q, k, v, out, scale
        self.bias, self.mask, self.sink, self.blocks, self.needs = bias, mask, sink, blocks, list(needs)
        n = heads * TT
        self.n = n
        self.b = m.scored.reserve(n)
        assert self.b % 2 == 0
        self.h0 = m.head_out.reserve(heads)
        self.s0, self.splits_n = m.splits.reserve(splits), splits
        self.t0 = m.tiles
        self.splits_per = 0

    def tensor(self, e):
        m = self.m
        for sem, value in self.needs:
            e.wait_ge(sem, value)
        m.wait_tiles(e, self.t0)
        for x in range(self.n + 3):
            if x < self.n:
                h, n = divmod(x, TT)
                if self.b + x > 1:
                    e.wait_ge(m.exped.sem if self.bias is None else m.maxed.sem, self.b + x - 1)
                kk = self.blocks(n) * P
                out = m.ps[:, 2 + x % 2, 0:kk]
                mm = e.matmul(out, self.q(h, n), self.k(h, n), start=True, stop=self.mask is None)
                if self.mask is not None:
                    mm = e.matmul(m.ps[:, 2 + x % 2, kk - P:kk], m.IDENTB[:], self.mask, start=False, stop=True)
                mm.then_inc(m.scored.sem, 1)
            if 2 <= x < self.n + 2:
                a = x - 2
                h, n = divmod(a, TT)
                e.wait_ge(m.normed.sem, self.b + a + 1)
                if self.b + a > 1:
                    e.wait_ge(m.turned.sem, self.b + a - 1)
                for j in range(self.blocks(n)):
                    mm = e.transpose(m.ps[:, 4 + a % 2, j * P:(j + 1) * P], self.buf.S[:, a % 3, j * P:(j + 1) * P], m.IDENT[:])
                mm.then_inc(m.flipped.sem, 1)
            if x >= 3:
                a = x - 3
                h, n = divmod(a, TT)
                e.wait_ge(m.turned.sem, self.b + a + 1)
                if n == 0 and self.h0 + h > 1:
                    e.wait_ge(m.head_out.sem, self.h0 + h - 1)
                p0 = HD * (h % 2)
                nb = self.blocks(n)
                for j in range(nb):
                    mm = e.matmul(m.ps[p0:p0 + HD, 6 + h % 2, n * P:(n + 1) * P], self.v(h, n, j),
                                  self.buf.PT[:, a % 2, j * P:(j + 1) * P], start=(j == 0), stop=(j == nb - 1))
                mm.then_inc(m.valued.sem, 1)

    def vector(self, e):
        m, v, B = self.m, self.m.vec, self.buf
        self.i = self.si = 0
        for x in range(self.n + 4):
            if x < self.n:
                h, n = divmod(x, TT)
                kk = self.blocks(n) * P
                c = x % 4
                e.wait_ge(m.scored.sem, self.b + x + 1)
                ps = m.ps[:, 2 + x % 2, 0:kk]
                if self.bias is not None:
                    if x > 2:
                        e.wait_ge(m.flipped.sem, self.b + x - 2)
                    e.tensor_tensor_reduce(B.S[:, x % 3, 0:kk], ps, self.bias(h, n), 1.0, -3e38, ALU.add,
                                           ALU.max, B.MX[:, c:c + 1]).then_inc(*v.next())
                else:
                    e.tensor_reduce(B.MX[:, c:c + 1], ps, AX.X, ALU.max).then_inc(*v.next())
                maximum = v.last
            if 1 <= x <= self.n:
                r = (x - 1) % 4
                e.wait_ge(m.exped.sem, self.b + x)
                if self.sink is not None:
                    e.tensor_tensor(B.RS[:, r:r + 1], B.RS[:, r:r + 1], B.ES[:, r:r + 1], ALU.add).then_inc(*v.next())
                    if x == self.n:
                        e.wait_ge(*v.last)
            if x < self.n:
                e.wait_ge(*maximum)
                if self.sink is not None:
                    e.tensor_scalar(B.NM[:, c:c + 1], B.MX[:, c:c + 1], self.sink(h), -self.scale, ALU.max,
                                    ALU.mult).then_inc(*v.gives(m.maxed.sem, self.b + x + 1))
                else:
                    e.tensor_scalar(B.NM[:, c:c + 1], B.MX[:, c:c + 1], -self.scale, None,
                                    ALU.mult).then_inc(*v.gives(m.maxed.sem, self.b + x + 1))
            if 1 <= x <= self.n:
                a = x - 1
                kk = self.blocks(a % TT) * P
                if self.sink is not None:
                    e.wait_ge(v.sem, v.n)
                e.reciprocal(B.RI[:, r:r + 1], B.RS[:, r:r + 1]).then_inc(*v.next())
                e.wait_ge(*v.last)
                e.tensor_scalar(B.S[:, a % 3, 0:kk], B.S[:, a % 3, 0:kk], B.RI[:, r:r + 1], None,
                                ALU.mult).then_inc(*v.gives(m.normed.sem, self.b + a + 1))
            if x >= 4 and (x - 4) % TT == TT - 1:
                h = (x - 4) // TT
                e.wait_ge(m.valued.sem, self.b + x - 3)
                p0 = HD * (h % 2)
                self.freed = (m.head_out.sem, self.h0 + h + 1)
                self.out(self, e, h, m.ps[p0:p0 + HD, 6 + h % 2, :], p0)
        e.wait_ge(*v.last)

    def scalar(self, e):
        m, B = self.m, self.buf
        for x in range(self.n + 2):
            if x < self.n:
                h, n = divmod(x, TT)
                kk = self.blocks(n) * P
                c = x % 4
                e.wait_ge(m.maxed.sem, self.b + x + 1)
                if self.bias is None and x > 2:
                    e.wait_ge(m.flipped.sem, self.b + x - 2)
                src = m.ps[:, 2 + x % 2, 0:kk] if self.bias is None else B.S[:, x % 3, 0:kk]
                if self.sink is not None:
                    e.activation(B.ES[:, c:c + 1], self.sink(h), ACT.Exp, bias=B.NM[:, c:c + 1], scale=self.scale)
                e.activation(B.S[:, x % 3, 0:kk], src, ACT.Exp, bias=B.NM[:, c:c + 1], scale=self.scale,
                             accum_out=B.RS[:, c:c + 1]).then_inc(m.exped.sem, 1)
            if x >= 2:
                a = x - 2
                kk = self.blocks(a % TT) * P
                e.wait_ge(m.flipped.sem, self.b + a + 1)
                if self.b + a > 1:
                    e.wait_ge(m.valued.sem, self.b + a - 1)
                e.activation(B.PT[:, a % 2, 0:kk], m.ps[:, 4 + a % 2, 0:kk], ACT.Copy).then_inc(m.turned.sem, 1)

    split = Gemm.split
    frees = Gemm.frees


class Buf:
    pass


def vector_rows():
    rows, at_ = [], {}

    def put(name, arg, n):
        at_[name] = len(rows)
        rows.extend((arg, r) for r in range(n))
    put("g_ff1", "g_ff1", 2 * DC)
    put("g_mix", "g_mix", 2 * DC)
    put("g_ff2", "g_ff2", 2 * DC)
    put("g_ple", "g_ple", 2 * DC)
    put("g_final", "g_final", DC)
    put("g_conv", "g_conv", 2 * CC)
    put("conv_b", "conv_b", 2 * CC)
    put("pre_norm", "pre_norm_2", 4 * DC)
    at_["_0"] = len(rows)
    put("post_norm", "post_norm_2", 4 * DC)
    put("a_d", "a_d_2", DC)
    put("a_b_glu", "a_b_glu_2", DC)
    put("c_q_norm", "c_q_norm_2", 6)
    put("c_kv_norm", "c_kv_norm_2", 2)
    put("d_ln_g", "d_ln_g_2", DC)
    put("d_ln_b", "d_ln_b_2", DC)
    put("lam_re", "lam_re", ST)
    at_["_1"] = len(rows)
    put("lam_im", "lam_im", ST)
    put("log_dt", "log_dt", ST)
    at_["_1b"] = len(rows)
    put("conv_w0", "conv_w0", CONV_K * CC)
    at_["_2"] = len(rows)
    put("conv_w1", "conv_w1", CONV_K * CC)
    at_["_3"] = len(rows)
    return rows, at_


def build(nc, out, a):
    with ExitStack() as ctx:
        m = Machine(nc, ctx)
        FL, FE = m.T2[0:HEADS, :], m.T[0:HEADS, :]
        sem = lambda n: Signal(ctx.enter_context(nc.semaphore(n)))
        m.flips, m.flip_free = sem("flips"), sem("flip_free")
        m.ask, m.answer = sem("ask"), sem("answer")
        m.scored, m.maxed, m.exped, m.normed = sem("scored"), sem("maxed"), sem("exped"), sem("normed")
        m.flipped, m.turned, m.valued, m.head_out = sem("flipped"), sem("turned"), sem("valued"), sem("head_out")
        m.vec_mark = sem("vec_mark")
        m.tap_product = sem("tap_product")
        m.tap_sum = sem("tap_sum")
        m.x_new = sem("x_new")
        m.x_high = sem("x_high")
        m.x_squared = sem("x_squared")
        param_in = [ctx.enter_context(nc.semaphore(f"param_in{i}")) for i in range(5)]
        x_in = [ctx.enter_context(nc.semaphore(f"x_in{i}")) for i in range(TT)]
        const_in = ctx.enter_context(nc.semaphore("const_in"))
        ple_in = ctx.enter_context(nc.semaphore("ple_in"))
        params_set = ctx.enter_context(nc.semaphore("params_set"))
        stored = ctx.enter_context(nc.semaphore("stored"))

        def wait_tiles(e, t):
            e.wait_ge(m.acc_free[0], (t + 1) // 2 + 1)
            e.wait_ge(m.acc_free[1], t // 2 + 1)
        m.wait_tiles = wait_tiles
        sb = m.sb
        rows, col = vector_rows()
        PV = sb("PV", [P, len(rows)])
        IDENTB = m.IDENTB = sb("IDENTB", [P, P], BF16)
        MASKF = sb("MASKF", [P, P])
        MASKB = sb("MASKB", [P, P], BF16)
        BFC = sb("BFC", [HEADS, 2])
        B = Buf()
        B.MX, B.NM, B.RS, B.RI, B.ES = [sb(n, [P, 4]) for n in ("MX", "NM", "RSUM", "RINV", "ESINK")]

        def gcol(name, i):
            c = col[name]
            if isinstance(i, int):
                return PV[:, c + i:c + i + 1]
            return PV[:, bass.ds(i + c, 1)]

        with ExitStack() as ph:
            HH, HL = sb("HH", [P, FC, SEQ], F32R, ph), sb("HL", [P, FC, SEQ], F32R, ph)
        with ExitStack() as ph:
            STAGE = sb("STAGE", [P, 5, P], F32, ph)
            DTROW = sb("DTROW", [ST, 2], F32, ph)
            XIN = sb("XIN", [P, TT, D], F32, ph)
        with ExitStack() as ph:
            G = sb("G", [P, 2 * DC, SEQ], F32, ph)
            Y = sb("Y", [P, CC, SEQ], F32, ph)
            with ExitStack() as sub:
                YP = sb("YP", [P, CC, SEQ], F32, sub)
                QKV = sb("QKV", [P, 3 * CC, SEQ], F32, sub)
                CA = sb("CA", [P, CC, SEQ + CONV_K - 1], F32, sub)
                V = sb("V", [P, TT, ATTN], F32, sub)
                B.S, B.PT = sb("S", [P, 3, SEQ], F32, sub), sb("PT", [P, 2, SEQ], F32, sub)
                CUM = sb("CUM", [HEADS, SEQ], F32, sub)
            with ExitStack() as sub:
                MH, ML = sb("MH", [P, DC, SEQ], F32R, sub), sb("ML", [P, DC, SEQ], F32R, sub)
            with ExitStack() as sub:
                PH, PL = sb("PH", [P, 2, SEQ], F32R, sub), sb("PL", [P, 2, SEQ], F32R, sub)
                PST = sb("PST", [P, TT, PLE], F32, sub)
        with ExitStack() as ph:
            UF, ZG = sb("UF", [P, DC, SEQ], F32, ph), sb("ZG", [P, DC, SEQ], F32, ph)
            with ExitStack() as sub:
                BT = sb("BT", [P, 2, DC, P], F32, sub)
                CT = sb("CT", [P, 3, DC, P], F32, sub)
                PS_ = sb("PS_", [P, 4, SEQ], F32, sub)
                WI = sb("WI", [P, 2, 2, SEQ], F32, sub)
                WS = sb("WS", [P, 2, SEQ], F32, sub)
                QS = sb("QS", [P, 4, SEQ], F32, sub)
                CS = sb("CS", [P, 3, 2, SEQ], F32, sub)
                SP_ = sb("SP_", [P, 12, ST], F32, sub)
                TI = sb("TI", [P, SEQ], F32, sub)
                KONST = sb("KONST", [P, 4], F32, sub)
            with ExitStack() as sub:
                M2H, M2L = sb("M2H", [P, DC, SEQ], F32R, sub), sb("M2L", [P, DC, SEQ], F32R, sub)
        with ExitStack() as ph:
            QB, ZB = sb("QB", [P, DC, SEQ], F32, ph), sb("ZB", [P, DC, SEQ], F32, ph)
            YB = QB
            KB = sb("KB", [P, 3, SEQ], F32, ph)
            VB = sb("VB", [P, TT, P], F32, ph)
            BIAS = sb("BIAS", [P, SWA_HEADS, 2 * P], F32, ph)
            RELB = sb("RELB", [33, SWA_HEADS], F32, ph)
            HOT = sb("HOT", [33, 3 * P], F32, ph)
            BROW = sb("BROW", [SWA_HEADS, 3 * P], F32, ph)
            SINK = sb("SINK", [P, SWA_HEADS], F32, ph)
            B2 = Buf()
            B2.S, B2.PT = sb("S2", [P, 3, SEQ], F32, ph), sb("PT2", [P, 2, SEQ], F32, ph)
        with ExitStack() as ph:
            ZC = sb("ZC", [P, DC, SEQ], F32, ph)
            YC = sb("YC", [P, DC, SEQ], F32, ph)
            QM = YC
            U2H, U2L = sb("U2H", [P, DC, SEQ], F32R, ph), sb("U2L", [P, DC, SEQ], F32R, ph)
            KM = sb("KM", [P, DC, SEQ], F32, ph)
            VM = sb("VM", [P, TT, SEQ], F32, ph)
            RT = sb("RT", [P, SEQ], F32, ph)
            RQ, RK = sb("RQ", [P, SEQ], F32, ph), sb("RK", [P, SEQ], F32, ph)
            B3 = Buf()
            B3.S, B3.PT = sb("S3", [P, 3, SEQ], F32, ph), m.FUN
        for x in (B2, B3):
            x.MX, x.NM, x.RS, x.RI, x.ES = B.MX, B.NM, B.RS, B.RI, B.ES
        with ExitStack() as ph:
            VF, UG, ZD = [sb(n, [P, DC, SEQ], F32, ph) for n in ("VF", "UG", "ZD")]
            YD = VF
            VTOK = sb("VTOK", [P, TT, D], F32, ph)
            WT, WSG = sb("WT", [P, SGU_GROUPS, P], F32, ph), sb("WSG", [P, SGU_GROUPS, P], F32, ph)
            MS, MU, R2 = [sb(n, [P, SEQ], F32, ph) for n in ("MS", "MU", "R2")]
            TRI = sb("TRI", [P, P], F32, ph)
            SELG = sb("SELG", [SGU_GROUPS, D], F32, ph)
            BSG = sb("BSG", [SGU_GROUPS, P], F32, ph)
        with ExitStack() as ph:
            OUT = sb("OUT", [P, TT, D], F32, ph)
        U = (m.UH, m.UL)
        steps = []
        add = steps.append

        n_stage = [col["_0"], col["_1"] - col["_0"], 2 * ST, CONV_K * CC, CONV_K * CC]

        class Start(Step):
            def tensor(self, e):
                e.sem_inc(m.unit_done.sem, 1)

            def scalar(self, e):
                e.dma_start(m.IDENT[:], a["c_ident"]).then_inc(const_in, 16)
                e.dma_start(MASKF[:], a["c_mask"]).then_inc(const_in, 16)
                for l in range(2):
                    e.dma_start(BFC[:, l:l + 1], a["b_f"][l].rearrange("(h o) -> h o", o=1)).then_inc(const_in, 16)
                for t in range(TT):
                    e.dma_start(XIN[:, t, :], a["x"][0, t * P:(t + 1) * P, :]).then_inc(x_in[t], 16)
                e.sem_inc(m.act_out.sem, 2)
                e.wait_ge(m.raw_ready[0], 16)
                e.activation(m.WH[:, 0, 0:m.unit_k[0], :], m.RAW[:, 0, 0:m.unit_k[0], :], ACT.Copy).then_inc(m.high_ready.sem, 1)

            def gpsimd(self, e):
                e.sem_inc(m.low_ready.sem, RAW_SLOTS)
                r = 0
                for s, n in enumerate(n_stage):
                    done = 0
                    while done < n:
                        arg, first = rows[r]
                        k = 1
                        while done + k < n and rows[r + k] == (arg, first + k):
                            k += 1
                        if arg.startswith("conv_w"):
                            src = a["conv_w"][int(arg[-1])].rearrange("j (c p) -> (j c) p", p=P)
                        elif arg == "lam_re" or arg == "lam_im":
                            src = a[f"a_{arg}_2"][0].rearrange("(t g) s -> t (g s)", g=2)
                        elif arg == "log_dt":
                            e.dma_start(DTROW[:], a["a_log_dt_2"][0].rearrange("(t g) -> t g", g=2)).then_inc(param_in[s], 16)
                            done += k
                            r += k
                            continue
                        else:
                            src = a[arg]
                            if len(src.shape) == 1:
                                src = src.rearrange("(r p) -> r p", p=P)
                            else:
                                src = src.rearrange("l (r p) -> (l r) p", p=P)
                        e.dma_start(STAGE[done:done + k, s, :], src[first:first + k, :]).then_inc(param_in[s], 16)
                        done += k
                        r += k

            def vector(self, e):
                for b in range(2):
                    e.sem_inc(m.acc_free[b], 1)
                for t, val in ((m.ONES, 1.0), (m.SS, 0.0), (m.EPSC, EPS), (m.ZERO, 0.0)):
                    e.memset(t[:], val).then_inc(*m.vec.next())
                e.wait_ge(const_in, 16 * 4)
                e.tensor_copy(IDENTB[:], m.IDENT[:]).then_inc(*m.vec.next())
                e.tensor_copy(MASKB[:], MASKF[:]).then_inc(*m.vec.next())
                e.wait_ge(param_in[2], 32)
                e.tensor_copy(STAGE[ST:2 * ST, 2, :].rearrange("t (g s) -> t g s", g=2),
                                         DTROW[:].unsqueeze(2).to_broadcast([ST, 2, STATE])).then_inc(*m.vec.next())
                e.wait_ge(m.vec.sem, m.vec.n)
                e.sem_inc(params_set, 1)
        def n_dmas(s):
            lo = sum(n_stage[:s])
            part = rows[lo:lo + n_stage[s]]
            return sum(1 for i, r in enumerate(part) if i == 0 or part[i - 1] != (r[0], r[1] - 1))
        add(Start())

        def flip_params(s):
            lo, n = sum(n_stage[:s]), n_stage[s]

            def pe(e, bank):
                e.wait_ge(param_in[s], 16 * n_dmas(s))
                if s == 2:
                    e.wait_ge(params_set, 1)
                return e.transpose(bank[:, 0:n], STAGE[0:n, s, :], m.IDENT[0:n, 0:n])

            def vec(g, e, bank):
                e.tensor_copy(PV[:, lo:lo + n], bank[:, 0:n]).then_inc(*g.frees())
                e.wait_ge(*m.vec.last)
            return pe, vec

        first_gain = lambda c: ("g_ff1", c)

        def flip_x(c):
            def pe(e, bank):
                for t in range(TT):
                    if c == 0:
                        e.wait_ge(x_in[t], 16)
                    ins = e.transpose(bank[:, t * P:(t + 1) * P], XIN[:, t, c * P:(c + 1) * P], m.IDENT[:])
                return ins

            def vec(g, e, bank):
                e.tensor_copy(m.X[:, c, :], bank).then_inc(*g.frees())
                after_x(g, e, c, gcol(*first_gain(c)))
            return pe, vec
        u_ready = m.splits.total
        add(Flips(m, [flip_params(0)] + [flip_x(c) for c in range(DC)] + [flip_params(s) for s in range(1, 5)],
                  needs=[(const_in, 16 * 4)], splits=DC, squares=DC))

        def ffn(l, w_in, w_out, next_gain):
            nonlocal u_ready
            wi, wo = chunks(w_in[l]), chunks(w_out[l])
            tiles = []
            for p in range(2):
                def b_vec(g, e, i, ps, p=p):
                    v = m.vec
                    e.tensor_tensor(m.T[:], ps, m.R[:], ALU.mult).then_inc(*g.frees())
                    e.wait_ge(m.act_out.sem, g.a)
                    e.wait_ge(*v.last)
                    e.tensor_tensor(m.T2[:], m.T[:], m.FUN[:, (g.a0 + p) % 2, :], ALU.mult).then_inc(*v.next())
                    g.split(e, at(HH, i * 2 + p), at(HL, i * 2 + p), m.T2[:])
                for half in range(2):
                    src = lambda i, o=half * FF + p * P: wi[:, :, bass.ds(i * 2 * P + o, P)]
                    tiles.append(Tile([(src, DC, 0)], U,
                                      vec=b_vec if half else None,
                                      act=None if half else (lambda e, i, pre, fun: e.activation(fun, pre, ACT.Silu))))
            r = Root(m, D)
            g1 = Gemm(m, FC // 2, tiles, vec_per_iter=4, rhs_ready=u_ready, splits=2, root=r)
            add(g1)
            tiles = []
            ks = [6, 6, 5, 5]
            for p in range(2):
                units, k0 = [], 0
                for k in ks:
                    units.append((lambda i, k0=k0, k=k, p=p: wo[:, k0:k0 + k, bass.ds(i * 2 * P + p * P, P)], k, k0))
                    k0 += k
                tiles.append(Tile(units, (HH, HL), vec=lambda g, e, i, ps, p=p: g.residual(
                    e, i * 2 + p, ps, 0.5, gcol(*next_gain(i * 2 + p)))))
            g2 = Gemm(m, DC // 2, tiles, vec_per_iter=4, rhs_ready=g1.s0, splits=2, squares=2)
            add(g2)
            u_ready = g2.s0


        def mixer(l):
            nonlocal u_ready
            w = chunks(a["w_in"][l])
            V0, F0 = 2 * ATTN, 3 * ATTN
            C0 = F0 + HEADS
            GA0 = C0 + 2 * CONV_CH
            v = m.vec
            UNIT = RAW_SLOTS

            def keep(g, e, i, ps, c):
                e.tensor_tensor(at(QKV, i * UNIT + c), ps, m.R[:], ALU.mult).then_inc(*g.frees())
            add(Gemm(m, 3, [Tile([(lambda i, c=c: w[:, :, bass.ds(i * UNIT * P + c * P, P)], DC, 0)], U,
                                 vec=lambda g, e, i, ps, c=c: keep(g, e, i, ps, c)) for c in range(UNIT)],
                     rhs_ready=u_ready, root=Root(m, D)))
            add(Gemm(m, 1, [Tile([(lambda i: w[:, :, F0:C0], DC, 0)], U, cols=HEADS,
                                 vec=lambda g, e, i, ps: e.tensor_tensor(FL, ps, m.R[0:HEADS, :], ALU.mult).then_inc(*g.frees()))],
                     rhs_ready=u_ready))

            def decay(s, e):
                e.tensor_scalar(FL, FL, BFC[:, l:l + 1], None, ALU.add).then_inc(*v.next())
                e.wait_ge(*v.last)
                e.scalar_tensor_tensor(FE, FL, -1.0, FL, ALU.mult, ALU.min).then_inc(*s.asks_next())
                e.wait_ge(s.m.answer.sem, s.answered(0))
                e.tensor_scalar(FE, FE, 1.0, None, ALU.add).then_inc(*s.asks_next())
                e.wait_ge(s.m.answer.sem, s.answered(1))
                e.scalar_tensor_tensor(FL, FL, 0.0, FE, ALU.min, ALU.subtract).then_inc(*v.next())
                e.wait_ge(*v.last)
                e.tensor_tensor_scan(CUM[:], m.ONES[0:HEADS, 0:1].to_broadcast([HEADS, SEQ]), FL, 0.0,
                                            ALU.mult, ALU.add).then_inc(*v.next())
                e.memset(CA[:, :, 0:CONV_K - 1], 0.0).then_inc(*v.next())

            add(VectorStep(m, decay, asks=[lambda e: e.activation(FE, FE, ACT.Exp), lambda e: e.activation(FE, FE, ACT.Ln)]))

            def flip_v(t):
                def pe(e, bank):
                    for c in range(CC):
                        ins = e.transpose(bank[:, c * P:(c + 1) * P], QKV[:, 2 * CC + c, t * P:(t + 1) * P], m.IDENT[:])
                    return ins

                def vec(g, e, bank):
                    e.tensor_copy(V[:, t, :], bank).then_inc(*g.frees())
                return pe, vec
            add(Flips(m, [flip_v(t) for t in range(TT)]))

            tiles = []
            for c in range(2):
                def first_half(g, e, i, ps, c=c):
                    e.wait_ge(*v.last)
                    e.tensor_tensor(m.T[:], ps, m.R[:], ALU.mult).then_inc(*g.frees())
                    e.wait_ge(m.act_out.sem, g.a)
                    e.wait_ge(*v.last)
                    dst = CA[:, bass.ds(i * 2 + c, 1), CONV_K - 1:]
                    e.tensor_tensor(dst, m.T[:], m.FUN[:, (g.a0 + c) % 2, :], ALU.mult).then_inc(*v.next())
                for half in (1, 0):
                    tiles.append(Tile([(lambda i, o=C0 + half * CONV_CH + c * P: w[:, :, bass.ds(i * 2 * P + o, P)], DC, 0)], U,
                                      vec=None if half else first_half,
                                      act=(lambda e, i, pre, fun: e.activation(fun, pre, ACT.Sigmoid)) if half else None))
            add(Gemm(m, 2, tiles, vec_per_iter=2, rhs_ready=u_ready))

            DVE_TAPS = CONV_K - 2 * UNIT
            SIDE = CONV_K - DVE_TAPS
            taps = [range(n * DVE_TAPS // UNIT, (n + 1) * DVE_TAPS // UNIT) for n in range(UNIT)]
            prod0, sum0 = m.tap_product.reserve(CC * SIDE), m.tap_sum.reserve(CC * (SIDE - 1))
            glu_mark = m.vec_mark.reserve(1) + 1

            class GluDone(Step):
                def vector(self, e):
                    e.wait_ge(*v.last)
                    e.sem_inc(m.vec_mark.sem, 1)
            add(GluDone())

            def convolve(g, e, i, n):
                y = Y[:, i, :]
                for j in taps[n]:
                    src = CA[:, i, j:j + SEQ]
                    wj = gcol(f"conv_w{l}", i + j * CC)
                    e.wait_ge(*v.last)
                    if j == 0:
                        e.tensor_scalar(y, src, wj, gcol("conv_b", i + l * CC), ALU.mult, ALU.add).then_inc(*v.next())
                    else:
                        e.scalar_tensor_tensor(y, src, wj, y, ALU.mult, ALU.add).then_inc(*v.next())
                if n == UNIT - 1:
                    e.wait_ge(m.tap_sum.sem, sum0 + (i + 1) * (SIDE - 1))
                    e.wait_ge(*v.last)
                    e.tensor_tensor(y, y, YP[:, i, :], ALU.add).then_inc(*v.next())
                    g.square(e, y)

            class Gates(Gemm):
                def scalar_tail(self, e, _, tile):
                    i, n = divmod(tile, UNIT)
                    if tile == 0:
                        e.wait_ge(m.vec_mark.sem, glu_mark)
                    for k in (2 * n, 2 * n + 1):
                        j = DVE_TAPS + k
                        if k > 0 and sum0 + i * (SIDE - 1) + max(k - 2, 0) > 0:
                            e.wait_ge(m.tap_sum.sem, sum0 + i * (SIDE - 1) + max(k - 2, 0))
                        dst = (m.T, m.T2)[k % 2][:] if k > 0 else YP[:, i, :]
                        e.activation(dst, CA[:, i, j:j + SEQ], ACT.Copy, scale=gcol(f"conv_w{l}", i + j * CC)).then_inc(m.tap_product.sem, 1)

                def gpsimd(self, e):
                    super().gpsimd(e)
                    self.gpsimd_tail(e, 0, self.nu)

                def gpsimd_tail(self, e, _, unit):
                    if unit == 0:
                        return
                    i, n = divmod(unit - 1, UNIT)
                    y = YP[:, i, :]
                    for k in (2 * n, 2 * n + 1):
                        if k > 0:
                            e.wait_ge(m.tap_product.sem, prod0 + i * SIDE + k + 1)
                            if sum0 + i * (SIDE - 1) + k > 1:
                                e.wait_ge(m.tap_sum.sem, sum0 + i * (SIDE - 1) + k - 1)
                            e.tensor_tensor(y, y, (m.T, m.T2)[k % 2][:], ALU.add).then_inc(m.tap_sum.sem, 1)

                def vector_tail(self, e, _, tile):
                    convolve(self, e, *divmod(tile, UNIT))
            add(Gates(m, 1, [Tile([(lambda i, c=c: w[:, :, GA0 + c * P:GA0 + (c + 1) * P], DC, 0)], U,
                                  act=lambda e, i, pre, fun, c=c: e.activation(G[:, c, :], pre, ACT.Sigmoid))
                             for c in range(2 * DC)], rhs_ready=u_ready, squares=CC))

            def conv_out(s, e):
                for c in range(CC):
                    e.scalar_tensor_tensor(Y[:, c, :], Y[:, c, :], gcol("g_conv", c + l * CC), m.R[:], ALU.mult, ALU.mult).then_inc(*s.asks_next())
                for c in range(CC):
                    e.wait_ge(s.m.answer.sem, s.answered(c))
                    s.split(e, m.UH[:, CC + c, :], m.UL[:, CC + c, :], Y[:, c, :])
            co = VectorStep(m, conv_out, asks=[lambda e, c=c: e.activation(Y[:, c, :], Y[:, c, :], ACT.Silu) for c in range(CC)],
                            splits=CC, root=Root(m, CONV_CH))
            add(co)

            def decay_row(h):
                return QKV[:, 2 * CC + h, :] if h < CC else CA[:, h - CC, 0:SEQ]

            def flip_c(h):
                def pe(e, bank):
                    return e.matmul(bank, m.IDENT[0:HEADS, h:h + 1].to_broadcast([HEADS, P]), CUM[:], start=True, stop=True)

                def vec(g, e, bank):
                    e.tensor_scalar(decay_row(h), bank, -1.0 / HD ** -0.5, None, ALU.mult).then_inc(*g.frees())
                return pe, vec
            add(Flips(m, [flip_c(h) for h in range(HEADS)]))

            def head(buf_chunk, h, sl):
                p0 = HD * (h % 2)
                return QKV[p0:p0 + HD, buf_chunk + h // 2, sl]

            def out_head(g, e, h, ps, p0):
                c = h // 2
                e.wait_ge(*v.last)
                e.tensor_copy(m.UH[p0:p0 + HD, c, :], ps).then_inc(*v.next())
                e.wait_ge(*v.last)
                e.tensor_tensor(m.UL[p0:p0 + HD, c, :], ps, m.UH[p0:p0 + HD, c, :].bitcast(F32), ALU.subtract).then_inc(*g.frees())
            att = Attention(m, B, HEADS, q=lambda h, n: head(0, h, slice(n * P, (n + 1) * P)),
                            k=lambda h, n: head(CC, h, slice(0, (n + 1) * P)),
                            v=lambda h, n, j: V[:, j, h * HD:(h + 1) * HD],
                            out=out_head, scale=HD ** -0.5, bias=lambda h, n: decay_row(h)[:, 0:(n + 1) * P], mask=MASKB[:],
                            needs=[(m.flip_free.sem, m.flips.total)])
            add(att)

            wa, wc = chunks(a["w_attn_out"][l]), chunks(a["w_conv_out"][l])
            g_done = m.act_out.total
            tiles = []
            for c in range(2):
                def attn_part(g, e, i, ps, c=c):
                    e.wait_ge(*v.last)
                    e.tensor_tensor(m.T[:], ps, at(G, i * 2 + c), ALU.mult).then_inc(*g.frees())

                def conv_part(g, e, i, ps, c=c):
                    e.tensor_tensor(m.T2[:], ps, at(G, i * 2 + (DC + c)), ALU.mult).then_inc(*g.frees())
                    e.wait_ge(*v.last)
                    e.tensor_tensor(m.T2[:], m.T[:], m.T2[:], ALU.add).then_inc(*v.next())
                    g.split(e, at(MH, i * 2 + c), at(ML, i * 2 + c), m.T2[:])
                tiles.append(Tile([(lambda i, c=c: wa[:, :, bass.ds(i * 2 * P + c * P, P)], CC, 0)], U, vec=attn_part))
                tiles.append(Tile([(lambda i, c=c: wc[:, :, bass.ds(i * 2 * P + c * P, P)], CC, CC)], U, vec=conv_part))
            mg = Gemm(m, DC // 2, tiles, vec_per_iter=4, rhs_ready=co.s0 + CC - DC, splits=2)
            mg.needs = [(m.head_out.sem, att.h0 + HEADS)]
            add(mg)
            wo = chunks(a["w_out"][l])
            g2 = Gemm(m, 2, [Tile([(lambda i, c=c: wo[:, :, bass.ds(i * UNIT * P + c * P, P)], DC, 0)], (MH, ML),
                                  vec=lambda g, e, i, ps, c=c: g.residual(e, i * UNIT + c, ps, 1.0, gcol("g_ff2", i * UNIT + c + l * DC)))
                             for c in range(UNIT)], vec_per_iter=8, rhs_ready=mg.s0, splits=UNIT, squares=UNIT)
            add(g2)
            u_ready = g2.s0

        def ple(l):
            nonlocal u_ready
            v = m.vec
            wg, wp = chunks(a["w_ple_gate"][l]), chunks(a["w_ple_proj"][l])

            def flip_p(c):
                def pe(e, bank):
                    e.wait_ge(ple_in, 16 * (l + 1))
                    for t in range(TT):
                        ins = e.transpose(bank[:, t * P:(t + 1) * P], PST[:, t, c * P:(c + 1) * P], m.IDENT[:])
                    return ins

                def vec(g, e, bank):
                    e.wait_ge(*v.last)
                    e.tensor_copy(m.T[:], bank).then_inc(*g.frees())
                    g.split(e, PH[:, c, :], PL[:, c, :], m.T[:])
                return pe, vec
            class LoadP(Step):
                need = m.splits.total

                def gpsimd(self, e):
                    e.wait_ge(m.splits.sem, self.need)
                    e.dma_start(PST[:], a["p"][l, 0].rearrange("(t p) f -> p t f", p=P)).then_inc(ple_in, 16)
            add(LoadP())
            fl = Flips(m, [flip_p(c) for c in range(2)], splits=2)
            add(Gemm(m, 2, [Tile([(lambda i, c=c: wg[:, :, bass.ds(i * 4 * P + c * P, P)], DC, 0)], U,
                                 act=lambda e, i, pre, fun, c=c: e.activation(at(G, i * 4 + c), pre, ACT.Sigmoid))
                            for c in range(4)], rhs_ready=u_ready, root=Root(m, D)))
            gates = m.act_out.total
            fl.t0 = m.tiles
            add(fl)
            last = l == 1

            def proj(g, e, i, ps, c):
                e.wait_ge(m.act_out.sem, gates)
                e.wait_ge(*v.last)
                e.tensor_tensor(m.T[:], ps, at(G, i * 4 + c), ALU.mult).then_inc(*g.frees())
                e.wait_ge(*v.last)
                x = at(m.X, i * 4 + c)
                e.tensor_tensor(x, x, m.T[:], ALU.add).then_inc(*v.next())
                g.square(e, x)
                if not last:
                    g.split_gain(e, at(m.UH, i * 4 + c), at(m.UL, i * 4 + c), x, gcol("g_ff1", i * 4 + (c + DC)))
            gp = Gemm(m, 2, [Tile([(lambda i, c=c: wp[:, :, bass.ds(i * 4 * P + c * P, P)], 2, 0)], (PH, PL),
                                  vec=lambda g, e, i, ps, c=c: proj(g, e, i, ps, c)) for c in range(4)],
                      vec_per_iter=8 if last else 12, rhs_ready=fl.s0, splits=0 if last else 4, squares=4)
            add(gp)
            u_ready = gp.s0

        def first_block():
            for l in range(2):
                ffn(l, a["w_ff1_in"], a["w_ff1_out"], lambda c, l=l: ("g_mix", c + l * DC))
                mixer(l)
                ffn(l, a["w_ff2_in"], a["w_ff2_out"], lambda c, l=l: ("g_ple", c + l * DC))
                ple(l)

        v = m.vec

        class Load(Step):

            def __init__(self, pairs, extra=(), on_scalar=False):
                self.pairs, self.on_scalar = pairs, on_scalar
                self.need = [(m.squares.sem, m.squares.total), (m.splits.sem, m.splits.total)] + list(extra)

            def gpsimd(self, e):
                if not self.on_scalar:
                    self.issue(e)

            def scalar(self, e):
                if self.on_scalar:
                    self.issue(e)

            def issue(self, e):
                for sem, value in self.need:
                    e.wait_ge(sem, value)
                for dst, src, sem in self.pairs:
                    e.dma_start(dst, src).then_inc(sem, 16)

        def norm_into_x(gain, next_gain, y=None):
            nonlocal u_ready
            st = Renorm(m, gain, next_gain, y)
            u_ready = st.s0
            add(st)

        def scaled(dst):
            def vec(g, e, i, ps):
                e.tensor_tensor(dst(i), ps, m.R[:], ALU.mult).then_inc(*g.frees())
            return vec

        def by_four(w, first, n, vec=None, act=None, rhs=U, pre=None, **kw):
            return Gemm(m, n // 4, [Tile([(lambda i, c=c: w[:, :, bass.ds(i * 4 * P + (first + c * P), P)], DC, 0)], rhs,
                                         vec=vec and vec(c), act=act and act(c), pre=pre and pre(c)) for c in range(4)], **kw)

        def out_gemm(w, y, rhs, ready, needs=(), straight=False):
            def vec(c):
                def f(g, e, i, ps):
                    e.tensor_copy(at(y, i * 4 + c), ps).then_inc(*g.frees())
                    g.square(e, at(y, i * 4 + c))
                return f
            if straight:
                g = Gemm(m, 1, [Tile([(lambda i, c=c: w[:, :, c * P:(c + 1) * P], DC, 0)], rhs, vec=vec(c)) for c in range(DC)],
                         rhs_ready=ready, squares=DC)
            else:
                g = by_four(w, 0, DC, vec=vec, rhs=rhs, vec_per_iter=4, rhs_ready=ready, squares=4)
            g.needs = list(needs)
            add(g)

        def s5():
            nonlocal u_ready
            w = chunks(a["a_w_in_2"][0])
            LAM_RE, LAM_IM = PV[:, col["lam_re"]:col["lam_re"] + ST], PV[:, col["lam_im"]:col["lam_im"] + ST]
            LOG_DT = PV[:, col["log_dt"]:col["log_dt"] + ST]
            add(by_four(w, 0, DC, vec=lambda c: scaled(lambda i: at(UF, i * 4 + c)), rhs_ready=u_ready, root=Root(m, D)))
            BRAW = [QS[:, n, :].rearrange("p (t h) -> p t h", h=GROUP) for n in range(2)]
            CRAW = [WI[:, n, :, :].rearrange("p a b -> p (a b)").rearrange("p (c x s) -> p c x s", x=2, s=STATE) for n in range(2)]
            pairs = [(TI[:], a["c_time"].partition_broadcast(P), s5_in), (KONST[:], a["c_konst"], s5_in)]
            for n, part in enumerate(("re", "im")):
                pairs.append((BRAW[n], a[f"a_b_{part}_2"][0].rearrange("(t g) s h -> (g s) t h", g=2), s5_in))
                for x in range(2):
                    pairs.append((CRAW[n][:, :, x, :], a[f"a_c_{part}_2"][0].rearrange("(c g) h s -> (g h) c s", c=DC), s5_in))
            add(Load(pairs, on_scalar=True))
            S = lambda n: SP_[:, n, :]
            DT, MAG, CO, SI, FR, HI, LO, FRE, FIM, A, Bb, Cc_ = [S(n) for n in range(12)]

            def tt(e, o, x, y, op):
                e.tensor_tensor(o, x, y, op).then_inc(*v.next())
                e.wait_ge(*v.last)

            def ts(e, o, x, s1, s2, op0, op1):
                ins = e.tensor_scalar(o, x, s1, s2, op0, op1) if s2 is not None else e.tensor_scalar(o, x, s1, None, op0)
                ins.then_inc(*v.next())
                e.wait_ge(*v.last)

            def stt(e, o, x, s1, y, op0, op1):
                e.scalar_tensor_tensor(o, x, s1, y, op0, op1).then_inc(*v.next())
                e.wait_ge(*v.last)
            PI1, PI2, PI3 = 6.28125, 1.93500518798828125e-3, TWO_PI - 6.28125 - 1.93500518798828125e-3

            def prepare(s, e):
                e.wait_ge(s5_in, 16 * len(pairs))
                e.tensor_copy(A, LOG_DT).then_inc(*s.asks_next())
                e.wait_ge(s.m.answer.sem, s.answered(0))
                e.tensor_tensor(A, LAM_RE, DT, ALU.mult).then_inc(*s.asks_next())
                tt(e, Bb, LAM_IM, DT, ALU.mult)
                ts(e, Cc_, Bb, 1.0 / TWO_PI, ROUND, ALU.mult, ALU.add)
                ts(e, Cc_, Cc_, -ROUND, None, ALU.add, None)
                yield
                stt(e, Bb, Cc_, -PI1, Bb, ALU.mult, ALU.add)
                stt(e, Bb, Cc_, -PI2, Bb, ALU.mult, ALU.add)
                stt(e, Bb, Cc_, -PI3, Bb, ALU.mult, ALU.add)
                ts(e, FR, Bb, 1.0 / TWO_PI, None, ALU.mult, None)
                ts(e, HI, FR, 32768.0, ROUND, ALU.mult, ALU.add)
                ts(e, HI, HI, -ROUND, 1.0 / 32768.0, ALU.add, ALU.mult)
                tt(e, LO, FR, HI, ALU.subtract)
                yield
                e.wait_ge(s.m.answer.sem, s.answered(1))
                ts(e, Bb, Bb, float(np.float32(3.1415925)), -float(np.float32(3.1415925)), ALU.min, ALU.max)
                e.tensor_copy(SI, Bb).then_inc(*s.asks_next())
                e.wait_ge(s.m.answer.sem, s.answered(2))
                e.tensor_scalar(CO, Bb, 1.0, None, ALU.mult).then_inc(*s.asks_next())
                e.wait_ge(s.m.answer.sem, s.answered(3))
                e.tensor_scalar(CO, CO, 1.0, None, ALU.mult).then_inc(*s.asks_next())
                e.wait_ge(s.m.answer.sem, s.answered(4))
                yield
                tt(e, A, MAG, CO, ALU.mult)
                ts(e, A, A, -1.0, None, ALU.add, None)
                tt(e, Bb, MAG, SI, ALU.mult)
                tt(e, CO, LAM_RE, LAM_RE, ALU.mult)
                tt(e, SI, LAM_IM, LAM_IM, ALU.mult)
                tt(e, CO, CO, SI, ALU.add)
                e.reciprocal(CO, CO).then_inc(*v.next())
                e.wait_ge(*v.last)
                yield
                tt(e, FRE, A, LAM_RE, ALU.mult)
                tt(e, Cc_, Bb, LAM_IM, ALU.mult)
                tt(e, FRE, FRE, Cc_, ALU.add)
                tt(e, FRE, FRE, CO, ALU.mult)
                tt(e, FIM, Bb, LAM_RE, ALU.mult)
                tt(e, Cc_, A, LAM_IM, ALU.mult)
                tt(e, FIM, FIM, Cc_, ALU.subtract)
                tt(e, FIM, FIM, CO, ALU.mult)
                yield
                bc = lambda x: x.unsqueeze(2).to_broadcast([P, ST, GROUP])
                T1, T2_ = [b[:].rearrange("p (t h) -> p t h", h=GROUP) for b in (m.T, m.T2)]
                e.memset(BD, 0.0).then_inc(*v.next())
                for n in range(2):
                    yield
                    f0, f1 = (FRE, FIM) if n == 0 else (FIM, FRE)
                    tt(e, T1, BRAW[0], bc(f0), ALU.mult)
                    tt(e, T2_, BRAW[1], bc(f1), ALU.mult)
                    tt(e, T1, T1, T2_, ALU.subtract if n == 0 else ALU.add)
                    for g in range(2):
                        e.tensor_copy(BD[HD * g:HD * (g + 1), n, :, GROUP * g:GROUP * (g + 1)], T1[HD * g:HD * (g + 1)]).then_inc(*v.next())
                        e.wait_ge(*v.last)
                    for x in range(2):
                        ts(e, CRAW[n][:, :, x, :], CRAW[n][:, :, x, :], KONST[:, x:x + 1], None, ALU.mult, None)
            BD = CS[:, 0:2, :, :].rearrange("p n a b -> p n (a b)").rearrange("p n (t x) -> p n t x", x=2 * GROUP)
            work = VectorStep(m, prepare, asks=[
                lambda e: e.activation(DT, A, ACT.Exp),
                lambda e: e.activation(MAG, A, ACT.Exp),
                lambda e: e.activation(SI, SI, ACT.Sin),
                lambda e: e.activation(CO, CO, ACT.Abs),
                lambda e: e.activation(CO, CO, ACT.Sin, bias=KONST[:, 2:3], scale=-1.0)])
            asks_of = {0: (0, 1), 2: (2, 3, 4)}

            class GateAndPrepare(Gemm):
                def scalar_tail(self, e, _, tile):
                    for n in asks_of.get(tile, ()):
                        e.wait_ge(m.ask.sem, work.a0 + n + 1)
                        work.asks[n](e).then_inc(m.answer.sem, 1)

                def vector(self, e):
                    work.asked = 0
                    self.parts = prepare(work, e)
                    super().vector(e)
                    for _ in self.parts:
                        pass

                def vector_tail(self, e, _, tile):
                    e.wait_ge(*v.last)
                    next(self.parts, None)
            add(GateAndPrepare(m, 1, [Tile([(lambda i, c=c: w[:, :, D + c * P:D + (c + 1) * P], DC, 0)], U,
                                           act=lambda e, i, pre, fun, c=c: e.activation(ZG[:, c, :], pre, ACT.Silu)) for c in range(DC)],
                               rhs_ready=u_ready))

            def flip_b(n, c0):
                def pe(e, bank):
                    e.wait_ge(m.vec_mark.sem, mark_b)
                    for c in range(4):
                        src = BD[:, n, (c0 + c) * 4:(c0 + c) * 4 + 4, :].rearrange("p t x -> p (t x)")
                        ins = e.transpose(bank[:, c * P:(c + 1) * P], src, m.IDENT[:])
                    return ins

                def vec(g, e, bank):
                    e.tensor_copy(BT[:, n, c0:c0 + 4, :], bank.rearrange("p (c x) -> p c x", x=P)).then_inc(*g.frees())
                return pe, vec

            def flip_cm(n, c0):
                def pe(e, bank):
                    for c in range(4):
                        src = CRAW[n][:, c0 + c, :, :].rearrange("p x s -> p (x s)")
                        ins = e.transpose(bank[:, c * P:(c + 1) * P], src, m.IDENT[:])
                    return ins

                def vec(g, e, bank):
                    b3 = bank.rearrange("p (c x) -> p c x", x=P)
                    if n == 0:
                        e.tensor_copy(CT[:, 0, c0:c0 + 4, :], b3).then_inc(*v.next())
                        e.tensor_scalar(CT[:, 1, c0:c0 + 4, :], b3, -1.0, None, ALU.mult).then_inc(*g.frees())
                    else:
                        e.tensor_scalar(CT[:, 2, c0:c0 + 4, :], b3, -1.0, None, ALU.mult).then_inc(*g.frees())
                return pe, vec
            mark_b = m.vec_mark.reserve(1) + 1

            class Mark(Step):
                def vector(self, e):
                    e.wait_ge(*v.last)
                    e.sem_inc(m.vec_mark.sem, 1)
            add(Mark())
            add(Flips(m, [flip_b(n, c0) for n in range(2) for c0 in (0, 4)] + [flip_cm(n, c0) for n in range(2) for c0 in (0, 4)]))

            class Recur(Step):
                flips_done = m.flips.total
                gates = m.act_out.total

                def tensor(self, e):
                    e.wait_ge(m.flip_free.sem, self.flips_done)

                    def bu(t):
                        c, i = divmod(t, 4)
                        if t - 1 > 0:
                            e.wait_ge(rotated.sem, t - 1)
                        rows_ = slice(32 * i, 32 * i + 32)
                        for n in range(2):
                            mm = e.matmul(m.ps[:, 2 + 2 * (t % 2) + n, :], BT[rows_, n, c, :], UF[rows_, c, :], start=True, stop=True)
                        mm.then_inc(driven.sem, 1)

                    bu(0)
                    for t in range(ST + 1):
                        if t + 1 < ST:
                            bu(t + 1)
                        if t >= 1:
                            c, i = divmod(t - 1, 4)
                            rows_ = slice(32 * i, 32 * i + 32)
                            e.wait_ge(half_out.sem, t)
                            if i == 0:
                                if c - 1 > 0:
                                    e.wait_ge(chunk_out.sem, c - 1)
                            out_ = m.ps[rows_, 6 + c % 2, :]
                            e.matmul(out_, CT[:, 0, c, rows_], QS[:, 0, :], start=True, stop=False)
                            e.wait_ge(other_out.sem, t)
                            e.matmul(out_, CT[:, 1, c, rows_], QS[:, 1, :], start=False, stop=False)
                            e.matmul(out_, CT[:, 2, c, rows_], QS[:, 2, :], start=False, stop=False)
                            e.matmul(out_, CT[:, 2, c, rows_], QS[:, 3, :], start=False, stop=True).then_inc(summed.sem, 1)

                def scalar(self, e):
                    def turns(t):
                        e.activation(m.PRE[:, t % 2, :], TI[:], ACT.Copy, scale=SP_[:, 5, t:t + 1]).then_inc(turned_by.sem, 1)
                    e.wait_ge(m.vec_mark.sem, mark_b)
                    e.wait_ge(m.act_out.sem, self.gates)
                    turns(0)
                    turns(1)
                    for t in range(ST):
                        e.wait_ge(phased.sem, t + 1)
                        if t + 2 < ST:
                            turns(t + 2)
                        if t >= 3:
                            e.wait_ge(other_out.sem, t - 2)
                            e.wait_ge(half_out.sem, t - 2)
                        e.activation(CS[:, t % 3, 1, :], m.FUN[:, t % 2, :], ACT.Sin, scale=6.283185)
                        e.activation(m.FUN[:, t % 2, :], m.FUN[:, t % 2, :], ACT.Abs).then_inc(*m.sca.next())
                        e.wait_ge(*m.sca.last)
                        e.activation(CS[:, t % 3, 0, :], m.FUN[:, t % 2, :], ACT.Sin, bias=KONST[:, 2:3], scale=-6.283185).then_inc(tabled.sem, 1)

                def vector(self, e):
                    def phase(t):
                        if t - 1 > 0:
                            e.wait_ge(tabled.sem, t - 1)
                        e.wait_ge(turned_by.sem, t + 1)
                        lo = SP_[:, 6, t:t + 1]
                        f = m.FUN[:, t % 2, :]
                        for low in (False, True):
                            src = m.T[:] if low else m.PRE[:, t % 2, :]
                            if low:
                                e.scalar_tensor_tensor(m.T[:], TI[:], lo, m.T[:], ALU.mult, ALU.add).then_inc(*v.next())
                            e.wait_ge(*v.last)
                            e.tensor_scalar(f, src, ROUND, -ROUND, ALU.add, ALU.add).then_inc(*v.next())
                            e.wait_ge(*v.last)
                            if low:
                                e.tensor_tensor(f, m.T[:], f, ALU.subtract).then_inc(*v.gives(phased.sem, t + 1))
                            else:
                                e.tensor_tensor(m.T[:], src, f, ALU.subtract).then_inc(*v.next())
                            e.wait_ge(*v.last)
                    phase(0)
                    for t in range(ST + 1):
                        if t + 1 < ST:
                            phase(t + 1)
                        if t < ST:
                            e.wait_ge(driven.sem, t + 1)
                            e.wait_ge(tabled.sem, t + 1)
                            if t > 0:
                                e.wait_ge(gathered.sem, t)
                            co, si = CS[:, t % 3, 0, :], CS[:, t % 3, 1, :]
                            bre, bim = m.ps[:, 2 + 2 * (t % 2), :], m.ps[:, 3 + 2 * (t % 2), :]
                            e.tensor_tensor(PS_[:, 0, :], bre, co, ALU.mult)
                            e.tensor_tensor(PS_[:, 1, :], bim, si, ALU.mult)
                            e.tensor_tensor(PS_[:, 2, :], bim, co, ALU.mult)
                            e.tensor_tensor(PS_[:, 3, :], bre, si, ALU.mult).then_inc(*v.gives(rotated.sem, t + 1))
                        if t >= 1:
                            x = t - 1
                            e.wait_ge(gathered.sem, x + 1)
                            if x > 0:
                                e.wait_ge(other_out.sem, x)
                            e.wait_ge(*v.last)
                            mag = MAG[:, x:x + 1].to_broadcast([P, SEQ])
                            for n in range(2):
                                e.tensor_tensor_scan(WS[:, n, :], mag, WI[:, x % 2, n, :], 0.0, ALU.mult, ALU.add).then_inc(*v.next())
                            e.wait_ge(*v.last)
                            e.sem_inc(scanned.sem, 1)
                            if x > 0:
                                e.wait_ge(summed.sem, x)
                            e.tensor_tensor(QS[:, 0, :], WS[:, 0, :], CS[:, x % 3, 0, :], ALU.mult).then_inc(*v.gives(half_out.sem, x + 1))
                        if t >= 2 and (t - 2) % 4 == 3:
                            chunk(e, (t - 2) // 4)
                    e.wait_ge(summed.sem, ST)
                    chunk(e, DC - 1)
                    e.wait_ge(*v.last)

            def chunk(e, c):
                e.wait_ge(summed.sem, 4 * c + 4)
                e.wait_ge(*v.last)
                e.scalar_tensor_tensor(UF[:, c, :], UF[:, c, :], gcol("a_d", c), m.ps[:, 6 + c % 2, :], ALU.mult, ALU.add).then_inc(*v.gives(chunk_out.sem, c + 1))

            def pool(self, e):
                for t in range(ST + 1):
                    if t < ST:
                        e.wait_ge(rotated.sem, t + 1)
                        if t - 1 > 0:
                            e.wait_ge(scanned.sem, t - 1)
                        e.tensor_tensor(WI[:, t % 2, 0, :], PS_[:, 0, :], PS_[:, 1, :], ALU.add)
                        e.tensor_tensor(WI[:, t % 2, 1, :], PS_[:, 2, :], PS_[:, 3, :], ALU.subtract).then_inc(gathered.sem, 1)
                    if t >= 1:
                        x = t - 1
                        e.wait_ge(scanned.sem, x + 1)
                        if x > 0:
                            e.wait_ge(summed.sem, x)
                        e.tensor_tensor(QS[:, 1, :], WS[:, 1, :], CS[:, x % 3, 1, :], ALU.mult)
                        e.tensor_tensor(QS[:, 2, :], WS[:, 0, :], CS[:, x % 3, 1, :], ALU.mult)
                        e.tensor_tensor(QS[:, 3, :], WS[:, 1, :], CS[:, x % 3, 0, :], ALU.mult).then_inc(other_out.sem, 1)
            Recur.gpsimd = pool
            add(Recur())

            def gelu(s, e):
                for c in range(DC):
                    e.wait_ge(m.answer.sem, s.k0 + c + 1)
                    s.split(e, m.UH[:, c, :], m.UL[:, c, :], UF[:, c, :])
            class Gelu(VectorStep):
                def scalar(self, e):
                    for c in range(DC):
                        e.wait_ge(chunk_out.sem, c + 1)
                        e.activation(UF[:, c, :], UF[:, c, :], ACT.Gelu_apprx_tanh).then_inc(m.answer.sem, 1)
            ge = Gelu(m, gelu, splits=DC)
            ge.k0 = m.answer.reserve(DC)
            add(ge)

            def glu(c):
                def f(g, e, i, ps):
                    e.wait_ge(*v.last)
                    e.tensor_tensor(m.T2[:], at(UF, i * 4 + c), at(ZG, i * 4 + c), ALU.mult).then_inc(*v.next())
                    e.wait_ge(*v.last)
                    e.tensor_tensor(m.T2[:], m.T2[:], g.fun, ALU.mult).then_inc(*v.next())
                    g.split(e, at(M2H, i * 4 + c), at(M2L, i * 4 + c), m.T2[:])
                return f
            gg = by_four(chunks(a["a_w_glu_2"][0]), 0, DC, vec=glu,
                         act=lambda c: (lambda e, i, pre, fun: e.activation(fun, pre, ACT.Sigmoid)),
                         pre=lambda c: (lambda e, i, pre, ps: e.tensor_scalar(pre, ps, gcol("a_b_glu", i * 4 + c), None, ALU.add)),
                         vec_per_iter=12, rhs_ready=ge.s0, splits=4)
            add(gg)
            out_gemm(chunks(a["a_w_out_2"][0]), UF, (M2H, M2L), gg.s0)

        def gated_head(z, head0=0):
            def f(g, e, h, ps, p0):
                c = (head0 + h) // 2
                r = slice(p0, p0 + HD)
                e.wait_ge(*v.last)
                e.tensor_tensor(m.T[r, :], ps, z[r, c, :], ALU.mult).then_inc(*v.next())
                e.wait_ge(*v.last)
                e.tensor_copy(m.UH[r, c, :], m.T[r, :]).then_inc(*v.next())
                e.wait_ge(*v.last)
                e.tensor_tensor(m.UL[r, c, :], m.T[r, :], m.UH[r, c, :].bitcast(F32), ALU.subtract).then_inc(*g.frees())
            return f

        def swa():
            w = chunks(a["b_w_in_2"][0])
            KV0 = SWA_HEADS * HD
            VW0, ZW0 = KV0 + 2 * HD, KV0 + 4 * HD
            add(Load([(RELB[0:32, :], a["rel_bias_2"], swa_in), (RELB[32:33, :], a["c_masked"], swa_in), (HOT[:], a["c_hot"], swa_in),
                      (SINK[:], a["b_sinks_2"][0].partition_broadcast(P), swa_in)]))

            def pe(e, bank):
                e.wait_ge(swa_in, 64)
                return e.matmul(bank[0:SWA_HEADS, 0:3 * P], RELB[:], HOT[:], start=True, stop=True)

            def vec(g, e, bank):
                e.tensor_scalar(BROW[:], bank[0:SWA_HEADS, 0:3 * P], 8.0, None, ALU.mult).then_inc(*g.frees())
                e.wait_ge(*v.last)
                e.wait_ge(swa_in, 64)
                e.tensor_scalar(SINK[:], SINK[:], 8.0, None, ALU.mult).then_inc(*v.next())
            fb = Flips(m, [(pe, vec)])
            add(fb)

            class Skew(Step):

                def gpsimd(self, e):
                    e.wait_ge(m.flip_free.sem, fb.b + 1)
                    wide = 3 * P
                    e.dma_start(skew.rearrange("h q x -> h q x"), BROW[:].unsqueeze(1).to_broadcast([SWA_HEADS, P, wide])).then_inc(skewed, 16)
                    e.wait_ge(skewed, 16)
                    src = bass.AP(skew.tensor, P - 1, [[wide - 1, P], [P * wide, SWA_HEADS], [1, 2 * P]])
                    e.dma_start(BIAS[:], src).then_inc(skewed, 16)
            add(Skew())
            add(by_four(w, 0, DC, vec=lambda c: scaled(lambda i: at(QB, i * 4 + c)), rhs_ready=u_ready, root=Root(m, D)))
            tiles = [Tile([(lambda i, k=k: [w[:, :, KV0 + k * HD:KV0 + (k + 1) * HD]] * 2, DC, 0)], U, vec=scaled(lambda i, k=k: KB[:, k, :]), loads=2)
                     for k in range(2)]
            tiles.insert(0, Tile([(lambda i: w[:, :, VW0:VW0 + P], DC, 0)], U, vec=scaled(lambda i: KB[:, 2, :])))
            add(Gemm(m, 1, tiles, rhs_ready=u_ready))
            add(by_four(w, ZW0, DC, act=lambda c: (lambda e, i, pre, fun: e.activation(at(ZB, i * 4 + c), pre, ACT.Silu)),
                        rhs_ready=u_ready))

            def pe2(e, bank):
                for t in range(TT):
                    ins = e.transpose(bank[:, t * P:(t + 1) * P], KB[:, 2, t * P:(t + 1) * P], m.IDENT[:])
                return ins
            fl = Flips(m, [(pe2, lambda g, e, bank: e.tensor_copy(VB[:], bank.rearrange("p (t x) -> p t x", x=P)).then_inc(*g.frees()))])
            add(fl)

            class WaitBias(Step):
                def vector(self, e):
                    e.wait_ge(skewed, 32)
                    e.wait_ge(m.act_out.sem, gates)
            gates = m.act_out.total
            add(WaitBias())
            first = lambda n: max(n - 1, 0) * P
            rows_ = lambda h: slice(HD * (h % 2), HD * (h % 2) + HD)
            nb = lambda n: 1 if n == 0 else 2
            att = Attention(m, B2, SWA_HEADS, q=lambda h, n: QB[rows_(h), h // 2, n * P:(n + 1) * P],
                            k=lambda h, n: KB[rows_(h), h // 8, first(n):(n + 1) * P],
                            v=lambda h, n, j: VB[:, max(n - 1, 0) + j, HD * (h // 8):HD * (h // 8) + HD],
                            out=gated_head(ZB), scale=HD ** -0.5, bias=lambda h, n: BIAS[:, h, P * (2 - nb(n)):2 * P],
                            sink=lambda h: SINK[:, h:h + 1], blocks=nb, needs=[(m.flip_free.sem, m.flips.total)])
            add(att)
            out_gemm(chunks(a["b_w_out_2"][0]), YB, U, m.splits.total - DC, needs=[(m.head_out.sem, m.head_out.total)])

        def mla():
            w = chunks(a["c_w_in_2"][0])
            wq, wkv = chunks(a["c_w_uq_2"][0]), chunks(a["c_w_ukv_2"][0])
            ROPE0 = Q_RANK + KV_RANK
            Z0 = ROPE0 + ROPE
            H2 = ROPE // 2
            top, swp = slice(NOPE, NOPE + ROPE), slice(NOPE + ROPE, NOPE + 2 * ROPE)
            add(Load([(RT[top, :], a["c_cos"], mla_in), (RT[swp, :], a["c_sin"], mla_in)]))

            def latent(c, gain):
                def f(g, e, i, ps):
                    e.wait_ge(*v.last)
                    e.tensor_tensor(m.T[:], ps, m.R[:], ALU.mult).then_inc(*g.frees())
                    g.square(e, m.T[:])
                    g.split_gain(e, U2H[:, c, :], U2L[:, c, :], m.T[:], gain)
                return f

            def tiles_of(lo, hi, name):
                return [Tile([(lambda i, c=c: w[:, :, c * P:(c + 1) * P], DC, 0)], U, vec=latent(c, gcol(name, c - lo)))
                        for c in range(lo, hi)]
            gq = Gemm(m, 1, tiles_of(0, 6, "c_q_norm"), rhs_ready=u_ready, splits=6, squares=6, root=Root(m, D))
            add(gq)
            gk = Gemm(m, 1, tiles_of(6, 8, "c_kv_norm"), rhs_ready=u_ready, splits=2, squares=2, root=Root(m, Q_RANK, dest=RQ))
            add(gk)

            def rope_k(g, e, i, ps):
                e.wait_ge(*v.last)
                e.wait_ge(mla_in, 32)
                e.tensor_tensor(m.T[top, :], ps[0:ROPE, :], RT[top, :], ALU.mult).then_inc(*v.next())
                e.wait_ge(*v.last)
                e.tensor_tensor(m.T2[top, :], ps[ROPE:2 * ROPE, :], RT[swp, :], ALU.mult).then_inc(*g.frees())
                e.wait_ge(*v.last)
                e.tensor_tensor(m.T[top, :], m.T[top, :], m.T2[top, :], ALU.add).then_inc(*v.next())
                e.wait_ge(*v.last)
                e.tensor_tensor(m.T[top, :], m.T[top, :], m.R[top, :], ALU.mult).then_inc(*v.next())
                e.wait_ge(*v.last)
                for h in range(8):
                    e.tensor_copy(KM[top, h, :], m.T[top, :]).then_inc(*v.next())
            add(Gemm(m, 1, [Tile([(lambda i: [w[:, :, ROPE0:Z0], w[:, :, ROPE0 + H2:Z0], w[:, :, ROPE0:ROPE0 + H2]], DC, 0)], U,
                                 cols=2 * ROPE, vec=rope_k, loads=3)], rhs_ready=u_ready, root=Root(m, KV_RANK, dest=RK)))
            add(by_four(w, Z0, DC, act=lambda c: (lambda e, i, pre, fun: e.activation(at(ZC, i * 4 + c), pre, ACT.Silu)),
                        rhs_ready=u_ready))

            class Tables(Step):
                def vector(self, e):
                    e.wait_ge(m.act_out.sem, self.gates)
                    e.wait_ge(*v.last)
                    both = slice(NOPE, NOPE + 2 * ROPE)
                    e.tensor_tensor(RT[both, :], RT[both, :], RQ[both, :], ALU.mult).then_inc(*v.next())
                    e.wait_ge(*v.last)
            tb = Tables()
            tb.gates = m.act_out.total
            add(tb)

            def query(h):
                def f(g, e, i, ps):
                    e.wait_ge(*v.last)
                    e.tensor_tensor(QM[0:NOPE, h, :], ps[0:NOPE, :], RQ[0:NOPE, :], ALU.mult).then_inc(*v.next())
                    e.tensor_tensor(m.T[top, :], ps[top, :], RT[top, :], ALU.mult).then_inc(*v.next())
                    e.tensor_tensor(m.T2[top, :], ps[swp, :], RT[swp, :], ALU.mult).then_inc(*g.frees())
                    e.wait_ge(*v.last)
                    e.tensor_tensor(QM[top, h, :], m.T[top, :], m.T2[top, :], ALU.add).then_inc(*v.next())
                return f
            VT = lambda k: (m.PRE if k < 2 else m.FUN)[:, k % 2, :]

            def key_value(h):
                def f(g, e, i, ps):
                    r = slice(HD * (h % 2), HD * (h % 2) + HD)
                    e.wait_ge(*v.last)
                    e.tensor_tensor(KM[0:NOPE, h, :], ps[0:NOPE, :], RK[0:NOPE, :], ALU.mult).then_inc(*v.next())
                    e.tensor_tensor(VT(h // 2)[r, :], ps[NOPE:2 * NOPE, :], RK[NOPE:2 * NOPE, :], ALU.mult).then_inc(*g.frees())
                return f
            for half in range(2):
                tiles = []
                for h in range(8):
                    q0 = (half * 8 + h) * QK
                    r0 = q0 + NOPE
                    kv0 = (half * 8 + h) * (NOPE + MLA_V)
                    tiles.append(Tile([(lambda i, kv0=kv0: wkv[:, :, kv0:kv0 + P], 2, 6)], (U2H, U2L), vec=key_value(h)))
                    tiles.append(Tile([(lambda i, q0=q0, r0=r0: [wq[:, :, q0:q0 + QK], wq[:, :, r0 + H2:r0 + ROPE], wq[:, :, r0:r0 + H2]], 6, 0)],
                                      (U2H, U2L), vec=query(h), loads=3))
                add(Gemm(m, 1, tiles, rhs_ready=gq.s0))

                def flip_v(t):
                    def pe(e, bank):
                        for k in range(4):
                            ins = e.transpose(bank[:, k * P:(k + 1) * P], VT(k)[:, t * P:(t + 1) * P], m.IDENT[:])
                        return ins
                    return pe, lambda g, e, bank: e.tensor_copy(VM[:, t, :], bank).then_inc(*g.frees())
                add(Flips(m, [flip_v(t) for t in range(TT)]))
                add(Attention(m, B3, 8, q=lambda h, n: QM[0:QK, h, n * P:(n + 1) * P], k=lambda h, n: KM[0:QK, h, 0:(n + 1) * P],
                              v=lambda h, n, j: VM[:, j, h * HD:(h + 1) * HD], out=gated_head(ZC, 8 * half), scale=QK ** -0.5,
                              mask=MASKB[:], needs=[(m.flip_free.sem, m.flips.total)]))
            out_gemm(chunks(a["c_w_out_2"][0]), YC, U, m.splits.total - DC, needs=[(m.head_out.sem, m.head_out.total)])

        def sgu():
            w = chunks(a["d_w_in_2"][0])
            add(Load([(WSG[:], a["d_w_s_2"][0].rearrange("g t s -> t g s"), sgu_in), (TRI[:], a["c_tri"], sgu_in),
                      (SELG[:], a["c_selg"], sgu_in), (BSG[:], a["d_b_s_2"][0], sgu_in)]))

            def v_tile(c):
                def f(g, e, i, ps):
                    x = at(VF, i * 4 + c)
                    e.wait_ge(*v.last)
                    e.tensor_tensor(MS[:], MS[:], x, ALU.add).then_inc(*v.next())
                    g.square(e, x)
                return f

            class Clear(Step):
                def vector(self, e):
                    e.wait_ge(*v.last)
                    e.memset(MS[:], 0.0).then_inc(*v.next())
                    e.wait_ge(*v.last)
            gelu = ACT.Gelu_apprx_tanh
            add(Clear())
            add(by_four(w, D, DC, vec=v_tile, act=lambda c: (lambda e, i, pre, fun: e.activation(at(VF, i * 4 + c), pre, gelu)),
                        vec_per_iter=8, rhs_ready=u_ready, squares=4, root=Root(m, D)))

            class Moments(Root):
                def tensor(self, e):
                    e.wait_ge(m.squares.sem, self.need)
                    e.matmul(m.ps[:, 6, :], m.ONES[:], MS[:], start=True, stop=True)
                    e.matmul(m.ps[:, 7, :], m.ONES[:], m.SS[:], start=True, stop=True).then_inc(m.stat.sem, 1)

                def vector(self, e):
                    pass

            def layer_norm(s, e):
                e.wait_ge(m.stat.sem, mo.b + 1)
                e.tensor_scalar(MU[:], m.ps[:, 6, :], 1.0 / D, None, ALU.mult).then_inc(*v.next())
                e.memset(m.SS[:], 0.0).then_inc(*v.next())
                e.wait_ge(*v.last)
                e.tensor_tensor(m.T[:], MU[:], MU[:], ALU.mult).then_inc(*v.next())
                e.wait_ge(*v.last)
                e.scalar_tensor_tensor(m.T[:], m.ps[:, 7, :], 1.0 / D, m.T[:], ALU.mult, ALU.subtract).then_inc(*s.asks_next())
                e.wait_ge(s.m.answer.sem, s.answered(0))
                e.reciprocal(R2[:], m.ROOT[:]).then_inc(*v.next())
                e.wait_ge(*v.last)
                for c in range(DC):
                    x = VF[:, c, :]
                    e.tensor_tensor(x, x, MU[:], ALU.subtract).then_inc(*v.next())
                    e.wait_ge(*v.last)
                    e.scalar_tensor_tensor(x, x, gcol("d_ln_g", c), R2[:], ALU.mult, ALU.mult).then_inc(*v.next())
                    e.wait_ge(*v.last)
                    e.tensor_scalar(x, x, gcol("d_ln_b", c), None, ALU.add).then_inc(*v.next())
                e.wait_ge(sgu_in, 64)
            mo = Moments(m, D)
            m.root.total -= 1
            mo.scalar = lambda e: None
            add(VectorStep(m, layer_norm, asks=[lambda e: e.activation(m.ROOT[:], m.T[:], ACT.Sqrt, bias=m.EPSC[:, 0:1])], root=mo))
            add(by_four(w, 0, DC, act=lambda c: (lambda e, i, pre, fun: e.activation(at(UG, i * 4 + c), pre, gelu)), rhs_ready=u_ready))

            def gate(c):
                def f(g, e, i, ps):
                    x = at(UG, i * 4 + c)
                    e.wait_ge(*v.last)
                    e.tensor_tensor(x, x, g.fun, ALU.mult).then_inc(*v.next())
                return f
            add(by_four(w, 2 * D, DC, vec=gate, act=lambda c: (lambda e, i, pre, fun: e.activation(fun, pre, ACT.Silu)),
                        vec_per_iter=4, rhs_ready=u_ready))

            def flip_w(g0):
                def pe(e, bank):
                    e.wait_ge(sgu_in, 64)
                    for g in range(4):
                        ins = e.transpose(bank[:, g * P:(g + 1) * P], WSG[:, g0 + g, :], m.IDENT[:])
                    return ins
                return pe, lambda s, e, bank: e.tensor_tensor(
                    WT[:, g0:g0 + 4, :], bank.rearrange("p (g t) -> p g t", t=P), TRI[:].unsqueeze(1).to_broadcast([P, 4, P]), ALU.mult).then_inc(*s.frees())

            def flip_v(t, c0):
                def pe(e, bank):
                    for c in range(4):
                        ins = e.transpose(bank[:, c * P:(c + 1) * P], VF[:, c0 + c, t * P:(t + 1) * P], m.IDENT[:])
                    return ins
                return pe, lambda s, e, bank: e.tensor_copy(VTOK[:, t, c0 * P:(c0 + 4) * P], bank).then_inc(*s.frees())
            mix_in = Flips(m, [flip_w(g0) for g0 in range(0, SGU_GROUPS, 4)] + [flip_v(t, c0) for t in range(TT) for c0 in (0, 4)])
            add(mix_in)

            def mix(c):
                def pe(e, bank):
                    e.matmul(bank, SELG[:, c * P:(c + 1) * P], BSG[:].unsqueeze(1).to_broadcast([SGU_GROUPS, TT, P]), start=True, stop=False,
                             skip_group_check=True)
                    for g in range(2):
                        for t in range(TT):
                            ins = e.matmul(bank[HD * g:HD * g + HD, t * P:(t + 1) * P], VTOK[:, t, (2 * c + g) * HD:(2 * c + g + 1) * HD],
                                           WT[:, 2 * c + g, :], start=False, stop=(g == 1 and t == TT - 1), skip_group_check=True)
                    return ins

                def vec(s, e, bank):
                    e.wait_ge(*v.last)
                    e.tensor_tensor(m.T[:], bank, UG[:, c, :], ALU.mult).then_inc(*s.frees())
                    s.split(e, m.UH[:, c, :], m.UL[:, c, :], m.T[:])
                return pe, vec
            mx = Flips(m, [mix(c) for c in range(DC)], needs=[(m.flip_free.sem, m.flips.total)], splits=DC)
            add(mx)
            out_gemm(chunks(a["d_w_out_2"][0]), YD, U, mx.s0, straight=True)

        s5_in, swa_in, mla_in, sgu_in, skewed = [ctx.enter_context(nc.semaphore(n)) for n in ("s5_in", "swa_in", "mla_in", "sgu_in", "skewed")]
        driven, rotated, gathered, scanned, half_out, other_out, summed, chunk_out, phased, tabled, turned_by = [sem(n) for n in (
            "driven", "rotated", "gathered", "scanned", "half_out", "other_out", "summed", "chunk_out", "phased", "tabled", "turned_by")]
        skew = nc.dram_tensor("skew", [SWA_HEADS, P, 3 * P], F32, kind="Internal").ap()

        def second_block():
            norm_into_x(lambda c: gcol("g_final", c), lambda c: gcol("pre_norm", c))
            kinds = [(s5, UF), (swa, YB), (mla, YC), (sgu, YD)]
            for n, (fn, y) in enumerate(kinds):
                fn()
                norm_into_x(lambda c, n=n: gcol("post_norm", n * DC + c),
                            (lambda c, n=n: gcol("pre_norm", (n + 1) * DC + c)) if n < 3 else None, y)
        first_block()
        second_block()
        finish(m, steps, out, OUT, stored)


def finish(m, steps, out, OUT, stored):
    nc = m.nc

    def store_x():
        x0 = m.x_new.total - DC

        def flip_out(t, c0):
            def pe(e, bank):
                e.wait_ge(m.x_new.sem, x0 + c0 + 4)
                for c in range(4):
                    ins = e.transpose(bank[:, c * P:(c + 1) * P], m.X[:, c0 + c, t * P:(t + 1) * P], m.IDENT[:])
                return ins
            return pe, lambda g, e, bank: e.tensor_copy(OUT[:, t, c0 * P:(c0 + 4) * P], bank).then_inc(*g.frees())
        parts = [(t, c0) for c0 in (0, 4) for t in range(TT)]
        fo = Flips(m, [flip_out(t, c0) for t, c0 in parts])
        steps.append(fo)

        class Store(Step):
            def sync(self, e):
                for n, (t, c0) in enumerate(parts):
                    e.wait_ge(m.flip_free.sem, fo.b + n + 1)
                    cols = slice(c0 * P, (c0 + 4) * P)
                    e.dma_start(out[0, t * P:(t + 1) * P, cols], OUT[:, t, cols]).then_inc(stored, 16)
                e.wait_ge(stored, 16 * len(parts))
        steps.append(Store())

    store_x()
    with nc.Block() as block:
        @block.sync
        def _(e):
            for s in steps:
                s.sync(e)

        @block.scalar
        def _(e):
            for s in steps:
                s.scalar(e)

        @block.gpsimd
        def _(e):
            for s in steps:
                s.gpsimd(e)

        @block.vector
        def _(e):
            for s in steps:
                s.vector(e)

        @block.tensor
        def _(e):
            for s in steps:
                s.tensor(e)


def constants():
    dist = 255 - np.arange(3 * P)
    ok = (dist >= 0) & (dist < WINDOW)
    far = 16 + np.floor(np.log(np.maximum(dist, 1) / 16.0) / np.log(8.0) * 16 + 1e-9).astype(np.int64)
    bucket = np.where(dist < 16, dist, np.minimum(far, 31))
    hot = np.zeros((33, 3 * P), np.float32)
    for x in range(3 * P):
        hot[bucket[x] if ok[x] else 32, x] = 1.0
    parity = (np.arange(P) // GROUP) % 2
    konst = np.zeros((P, 4), np.float32)
    konst[:, 0], konst[:, 1], konst[:, 2] = parity == 0, parity == 1, np.pi / 2
    inv = (np.float32(10000.0) ** (-np.arange(0, ROPE, 2, dtype=np.float32) / np.float32(ROPE))).astype(np.float32)
    ang = (np.arange(SEQ, dtype=np.float32)[None, :] * inv[:, None]).astype(np.float32)
    cos, sin = np.cos(ang).astype(np.float32), np.sin(ang).astype(np.float32)
    selg = (np.arange(D)[None, :] // HD == np.arange(SGU_GROUPS)[:, None]).astype(np.float32)
    return {"c_time": np.arange(SEQ, dtype=np.float32), "c_konst": konst, "c_hot": hot,
            "c_masked": np.full((1, SWA_HEADS), MASKED, np.float32),
            "c_cos": np.concatenate([cos, cos]), "c_sin": np.concatenate([-sin, sin]),
            "c_tri": (np.arange(P)[:, None] <= np.arange(P)[None, :]).astype(np.float32), "c_selg": selg,
            "c_ident": np.eye(P, dtype=np.float32),
            "c_mask": np.where(np.arange(P)[None] > np.arange(P)[:, None], np.float32(MASKED), np.float32(0))}


INPUTS = (
    "x", "p", "g_ff1", "w_ff1_in", "w_ff1_out", "g_mix", "w_in", "b_f", "w_attn_out", "conv_w", "conv_b",
    "g_conv", "w_conv_out", "w_out", "g_ff2", "w_ff2_in", "w_ff2_out", "g_ple", "w_ple_gate", "w_ple_proj",
    "g_final", "pre_norm_2", "post_norm_2", "rel_bias_2", "a_w_in_2", "a_lam_re_2", "a_lam_im_2",
    "a_log_dt_2", "a_b_re_2", "a_b_im_2", "a_c_re_2", "a_c_im_2", "a_d_2", "a_w_glu_2", "a_b_glu_2",
    "a_w_out_2", "b_w_in_2", "b_sinks_2", "b_w_out_2", "c_w_in_2", "c_q_norm_2", "c_kv_norm_2", "c_w_uq_2",
    "c_w_ukv_2", "c_w_out_2", "d_w_in_2", "d_ln_g_2", "d_ln_b_2", "d_w_s_2", "d_b_s_2", "d_w_out_2",
)


def kernel(**inputs):
    import concourse.bacc as bacc
    from concourse.bass_utils import run_bass_kernel_spmd

    nc = bacc.Bacc("TRN2", target_bir_lowering=False, num_devices=1)
    arrays = {name: np.ascontiguousarray(inputs[name]) for name in INPUTS}
    arrays.update(constants())
    aps = {name: nc.dram_tensor(name, array.shape, mybir.dt.from_np(array.dtype), kind="ExternalInput").ap()
           for name, array in arrays.items()}
    out = nc.dram_tensor("out", (1, SEQ, D), F32, kind="ExternalOutput").ap()
    build(nc, out, aps)
    result = run_bass_kernel_spmd(nc, [arrays], core_ids=[0])
    return result.results[0]["out"]
```
